# Optimizing a Trainium2 kernel written in Bass

```python
import math
import jax
import jax.numpy as jnp
from jax import lax
import numpy as np
import jax, jax.numpy as jnp

D_MODEL = 2048
BATCH = 1
SEQ = 256
DEPTH = 2

EPS = 1e-6

POOL_WINDOWS = (2, 4, 8, 16)
POOL_GROUPS = len(POOL_WINDOWS)
POOL_WIDTH = D_MODEL // 2
POOL_GC = POOL_WIDTH // POOL_GROUPS

DSA_HEADS = 16
DSA_HEAD_DIM = 64
DSA_WIDTH = DSA_HEADS * DSA_HEAD_DIM
IDX_HEADS = 16
IDX_DIM = 64
DSA_MAX_TOPK = 256
Q_BLOCK = 128

SWA_Q_HEADS = 32
SWA_KV_HEADS = 4
SWA_HEAD_DIM = 64
SWA_WIDTH = SWA_Q_HEADS * SWA_HEAD_DIM
WINDOW = 128

NUM_BUCKETS = 32
MAX_DISTANCE = 1024
BIAS_HEADS = 32

EVEN_SPLITS = (POOL_WIDTH, POOL_WIDTH,
               DSA_WIDTH, DSA_HEAD_DIM, DSA_HEAD_DIM,
               DSA_WIDTH,
               IDX_HEADS * IDX_DIM, IDX_DIM, IDX_HEADS)
EVEN_IN = sum(EVEN_SPLITS)
EVEN_OUT_IN = POOL_WIDTH + DSA_WIDTH
ODD_SPLITS = (SWA_WIDTH, SWA_KV_HEADS * SWA_HEAD_DIM, SWA_KV_HEADS * SWA_HEAD_DIM, SWA_WIDTH)
ODD_IN = sum(ODD_SPLITS)


def rms_norm(x, g):
    xf = x.astype(jnp.float32)
    y = xf * lax.rsqrt(jnp.mean(xf * xf, axis=-1, keepdims=True) + EPS) * g.astype(jnp.float32)
    return y.astype(x.dtype)

def split_cols(h, sizes):
    return jnp.split(h, np.cumsum(sizes)[:-1].tolist(), axis=-1)

def t5_bucket(n):
    n = jnp.maximum(n, 0)
    max_exact = NUM_BUCKETS // 2
    nf = jnp.maximum(n, 1).astype(jnp.float32)
    large = max_exact + (jnp.log(nf / max_exact) / math.log(MAX_DISTANCE / max_exact)
                         * (NUM_BUCKETS - max_exact)).astype(jnp.int32)
    large = jnp.minimum(large, NUM_BUCKETS - 1)
    return jnp.where(n < max_exact, n, large)

def causal_multiscale_pool(a):
    B, T, G, C = a.shape
    cs = jnp.cumsum(a.astype(jnp.float32), axis=1)
    csp = jnp.concatenate([jnp.zeros((B, 1, G, C), jnp.float32), cs], axis=1)
    t = jnp.arange(T)
    outs = []
    for g, w in enumerate(POOL_WINDOWS):
        lo = jnp.maximum(t + 1 - w, 0)
        s = csp[:, t + 1, g] - csp[:, lo, g]
        cnt = (t + 1 - lo).astype(jnp.float32)
        outs.append(s / cnt[None, :, None])
    return jnp.stack(outs, axis=2).astype(a.dtype)

def dsa_attention(q, k, v, iq, ik, iw, rel_bias, topk):
    B, T, H, d = q.shape
    nb = T // Q_BLOCK
    scale = DSA_HEAD_DIM ** -0.5
    keys = jnp.arange(T)

    def to_blocks(z):
        return jnp.swapaxes(z.reshape((B, nb, Q_BLOCK) + z.shape[2:]), 0, 1)

    def block_fn(args):
        qb, iqb, iwb, start = args
        pos_q = start + jnp.arange(Q_BLOCK)
        s_idx = jnp.einsum('bqhe,bse->bqhs', iqb, ik).astype(jnp.float32) * (IDX_DIM ** -0.5)
        score = jnp.einsum('bqhs,bqh->bqs', jax.nn.relu(s_idx), iwb.astype(jnp.float32))
        score = jnp.where(keys[None, None, :] <= pos_q[None, :, None], score, -jnp.inf)
        _, idx = lax.top_k(score, topk)
        valid = idx <= pos_q[None, :, None]
        kg = jax.vmap(lambda kk, ii: kk[ii])(k, idx)
        vg = jax.vmap(lambda vv, ii: vv[ii])(v, idx)
        logits = jnp.einsum('bqhd,bqkd->bhqk', qb, kg).astype(jnp.float32) * scale
        bias = rel_bias[t5_bucket(pos_q[None, :, None] - idx)][..., :H]
        logits = logits + jnp.transpose(bias, (0, 3, 1, 2)).astype(jnp.float32)
        logits = jnp.where(valid[:, None], logits, -jnp.inf)
        p = jax.nn.softmax(logits, axis=-1).astype(vg.dtype)
        return jnp.einsum('bhqk,bqkd->bqhd', p, vg)

    starts = jnp.arange(nb) * Q_BLOCK
    out = lax.map(block_fn, (to_blocks(q), to_blocks(iq), to_blocks(iw), starts))
    return jnp.swapaxes(out, 0, 1).reshape(B, T, H, d)

def swa_sink_attention(q, k, v, sinks, rel_bias):
    B, T, HQ, d = q.shape
    HKV = k.shape[2]
    G = HQ // HKV
    W = WINDOW
    nb = T // W
    qb = q.reshape(B, nb, W, HKV, G, d)

    def with_prev(z):
        zb = z.reshape(B, nb, W, HKV, d)
        prev = jnp.concatenate([jnp.zeros_like(zb[:, :1]), zb[:, :-1]], axis=1)
        return jnp.concatenate([prev, zb], axis=2)

    kw, vw = with_prev(k), with_prev(v)
    logits = jnp.einsum('bnqhgd,bnkhd->bnhgqk', qb, kw).astype(jnp.float32) * (d ** -0.5)
    i = jnp.arange(W)
    j = jnp.arange(2 * W)
    dist = W + i[:, None] - j[None, :]
    bias = rel_bias[t5_bucket(dist)][..., :HQ]
    bias = jnp.transpose(bias, (2, 0, 1)).reshape(HKV, G, W, 2 * W).astype(jnp.float32)
    in_window = (dist >= 0) & (dist < W)
    has_prev = (jnp.arange(nb)[:, None, None] > 0) | (j[None, None, :] >= W)
    mask = in_window[None] & has_prev
    logits = jnp.where(mask[None, :, None, None], logits + bias, -jnp.inf)
    sink = jnp.broadcast_to(sinks.astype(jnp.float32).reshape(HKV, G)[None, None, :, :, None, None],
                            (B, nb, HKV, G, W, 1))
    p = jax.nn.softmax(jnp.concatenate([logits, sink], axis=-1), axis=-1)[..., :-1]
    out = jnp.einsum('bnhgqk,bnkhd->bnqhgd', p.astype(vw.dtype), vw)
    return out.reshape(B, T, HQ * d)

def even_layer(x, norm_g, w_in, pool_w, pool_scale, q_gain, k_gain, w_out, rel_bias):
    B, T, _ = x.shape
    h = rms_norm(x, norm_g) @ w_in
    p_in, p_gate, dq, dk, dv, d_gate, iq, ik, iw = split_cols(h, EVEN_SPLITS)
    pa = p_in.reshape(B, T, POOL_GROUPS, POOL_GC)
    pooled = causal_multiscale_pool(pa) - pa
    py = jnp.einsum('btgc,gcd->btgd', pooled, pool_w) * pool_scale.reshape(POOL_GROUPS, POOL_GC)
    py = jax.nn.silu(p_gate) * py.reshape(B, T, POOL_WIDTH)
    q = rms_norm(dq.reshape(B, T, DSA_HEADS, DSA_HEAD_DIM), q_gain)
    k = rms_norm(dk, k_gain)
    iq = iq.reshape(B, T, IDX_HEADS, IDX_DIM)
    iw = iw * (IDX_HEADS ** -0.5)
    topk = min(DSA_MAX_TOPK, T // 4)
    o = dsa_attention(q, k, dv, iq, ik, iw, rel_bias, topk)
    dy = jax.nn.silu(d_gate) * o.reshape(B, T, DSA_WIDTH)
    return x + jnp.concatenate([py, dy], axis=-1) @ w_out

def odd_layer(x, norm_g, w_in, q_gain, k_gain, sinks, w_out, rel_bias):
    B, T, _ = x.shape
    h = rms_norm(x, norm_g) @ w_in
    q, k, v, gate = split_cols(h, ODD_SPLITS)
    q = rms_norm(q.reshape(B, T, SWA_Q_HEADS, SWA_HEAD_DIM), q_gain)
    k = rms_norm(k.reshape(B, T, SWA_KV_HEADS, SWA_HEAD_DIM), k_gain)
    v = v.reshape(B, T, SWA_KV_HEADS, SWA_HEAD_DIM)
    o = swa_sink_attention(q, k, v, sinks, rel_bias)
    return x + (jax.nn.silu(gate) * o) @ w_out

def first_inputs(seed: int = 0) -> dict:
    key = jax.random.key(seed)
    ks = jax.random.split(key, 16)
    n_even = (DEPTH + 1) // 2
    n_odd = DEPTH // 2
    nrm = jax.random.normal
    f32 = jnp.float32
    return {
        "x": nrm(ks[0], (BATCH, SEQ, D_MODEL), f32),
        "rel_bias": 0.5 * nrm(ks[1], (NUM_BUCKETS, BIAS_HEADS), f32),
        "even_norm": 1.0 + 0.02 * nrm(ks[2], (n_even, D_MODEL), f32),
        "even_w_in": nrm(ks[3], (n_even, D_MODEL, EVEN_IN), f32) * D_MODEL ** -0.5,
        "even_pool_w": nrm(ks[4], (n_even, POOL_GROUPS, POOL_GC, POOL_GC), f32) * POOL_GC ** -0.5,
        "even_pool_scale": 1.0 + 0.02 * nrm(ks[5], (n_even, POOL_WIDTH), f32),
        "even_q_gain": 1.0 + 0.02 * nrm(ks[6], (n_even, DSA_HEAD_DIM), f32),
        "even_k_gain": 1.0 + 0.02 * nrm(ks[7], (n_even, DSA_HEAD_DIM), f32),
        "even_w_out": nrm(ks[8], (n_even, EVEN_OUT_IN, D_MODEL), f32) * EVEN_OUT_IN ** -0.5,
        "odd_norm": 1.0 + 0.02 * nrm(ks[9], (n_odd, D_MODEL), f32),
        "odd_w_in": nrm(ks[10], (n_odd, D_MODEL, ODD_IN), f32) * D_MODEL ** -0.5,
        "odd_q_gain": 1.0 + 0.02 * nrm(ks[11], (n_odd, SWA_HEAD_DIM), f32),
        "odd_k_gain": 1.0 + 0.02 * nrm(ks[12], (n_odd, SWA_HEAD_DIM), f32),
        "odd_sinks": nrm(ks[13], (n_odd, SWA_Q_HEADS), f32),
        "odd_w_out": nrm(ks[14], (n_odd, SWA_WIDTH, D_MODEL), f32) * SWA_WIDTH ** -0.5,
    }

def first_block(x, rel_bias, even_norm, even_w_in, even_pool_w, even_pool_scale, even_q_gain,
              even_k_gain, even_w_out, odd_norm, odd_w_in, odd_q_gain, odd_k_gain, odd_sinks,
              odd_w_out):
    for layer in range(DEPTH):
        i = layer // 2
        if layer % 2 == 0:
            x = even_layer(x, even_norm[i], even_w_in[i], even_pool_w[i], even_pool_scale[i],
                           even_q_gain[i], even_k_gain[i], even_w_out[i], rel_bias)
        else:
            x = odd_layer(x, odd_norm[i], odd_w_in[i], odd_q_gain[i], odd_k_gain[i],
                          odd_sinks[i], odd_w_out[i], rel_bias)
    return x


DEPTH_2 = 1

N_HEADS = 8
HEAD_DIM = 128
ATTN_W = N_HEADS * HEAD_DIM
MOBA_BLOCK = 256
MOBA_TOPK = 3
MOBA_QCHUNK = 64
N_BUCKETS = 32
MAX_DISTANCE_2 = 128
LRU_W = D_MODEL // 2
LRU_BLOCKS = 8
LRU_BW = LRU_W // LRU_BLOCKS
LRU_CONV = 4
LRU_C = 8.0
SC_W = D_MODEL // 2
SC_CONV = 3
D_FF = 4 * D_MODEL
N_BRANCH = 3
IN_SPLITS = (ATTN_W, ATTN_W, ATTN_W, LRU_W, LRU_W, SC_W, SC_W, SC_W, N_BRANCH * D_MODEL)
N_IN = sum(IN_SPLITS)


def rms_norm_2(x, g):
    xf = x.astype(jnp.float32)
    y = xf * lax.rsqrt(jnp.mean(xf * xf, axis=-1, keepdims=True) + EPS)
    return (y * g.astype(jnp.float32)).astype(x.dtype)

def causal_depthwise_conv(x, w):
    k = w.shape[0]
    return lax.conv_general_dilated(
        x, w[:, None, :].astype(x.dtype), window_strides=(1,), padding=[(k - 1, 0)],
        dimension_numbers=('NWC', 'WIO', 'NWC'), feature_group_count=x.shape[-1])

def t5_bucket_2(dist):
    n = jnp.maximum(dist, 0)
    max_exact = N_BUCKETS // 2
    nf = jnp.maximum(n, 1).astype(jnp.float32)
    large = max_exact + (jnp.log(nf / max_exact) / math.log(MAX_DISTANCE_2 / max_exact)
                         * (N_BUCKETS - max_exact)).astype(jnp.int32)
    large = jnp.minimum(large, N_BUCKETS - 1)
    return jnp.where(n < max_exact, n, large)

def moba_attention(q, k, v, rel_table):
    bsz, seq, n_heads, d_head = q.shape
    n_blk = -(-seq // MOBA_BLOCK)
    s_pad = n_blk * MOBA_BLOCK
    topk = min(MOBA_TOPK, n_blk)
    pad = ((0, 0), (0, s_pad - seq), (0, 0), (0, 0))
    qh = jnp.pad(q * (d_head ** -0.5), pad).transpose(0, 2, 1, 3)
    kh = jnp.pad(k, pad).transpose(0, 2, 1, 3)
    vh = jnp.pad(v, pad).transpose(0, 2, 1, 3)
    kb = kh.reshape(bsz, n_heads, n_blk, MOBA_BLOCK, d_head)
    vb = vh.reshape(bsz, n_heads, n_blk, MOBA_BLOCK, d_head)
    k_mean = jnp.mean(kb.astype(jnp.float32), axis=3)
    gate = jnp.einsum('bhsd,bhnd->bhsn', qh.astype(jnp.float32), k_mean)
    q_blk = jnp.arange(s_pad) // MOBA_BLOCK
    past = jnp.arange(n_blk)[None, :] < q_blk[:, None]
    gate = jnp.where(past, gate, -jnp.inf)
    _, sel = lax.top_k(gate, topk)
    slot_ok = jnp.arange(topk)[None, :] < q_blk[:, None]
    b_idx = jnp.arange(bsz)[:, None, None, None]
    h_idx = jnp.arange(n_heads)[None, :, None, None]
    tbl_hb = rel_table.T
    blk_pos = jnp.arange(MOBA_BLOCK)

    def chunk(c):
        start = c * MOBA_QCHUNK
        qc = lax.dynamic_slice_in_dim(qh, start, MOBA_QCHUNK, axis=2)
        sel_c = lax.dynamic_slice_in_dim(sel, start, MOBA_QCHUNK, axis=2)
        ok_c = lax.dynamic_slice_in_dim(slot_ok, start, MOBA_QCHUNK, axis=0)
        q_pos = start + jnp.arange(MOBA_QCHUNK)
        kg = kb[b_idx, h_idx, sel_c]
        vg = vb[b_idx, h_idx, sel_c]
        s_past = jnp.einsum('bhqd,bhqnkd->bhqnk', qc, kg, preferred_element_type=jnp.float32)
        k_pos = sel_c[..., None] * MOBA_BLOCK + blk_pos
        bkt = t5_bucket_2(q_pos[:, None, None] - k_pos)
        s_past = s_past + tbl_hb[h_idx[..., None], bkt]
        s_past = jnp.where(ok_c[:, :, None], s_past, -jnp.inf)
        own = start // MOBA_BLOCK
        k_own = lax.dynamic_index_in_dim(kb, own, axis=2, keepdims=False)
        v_own = lax.dynamic_index_in_dim(vb, own, axis=2, keepdims=False)
        s_own = jnp.einsum('bhqd,bhkd->bhqk', qc, k_own, preferred_element_type=jnp.float32)
        dist = q_pos[:, None] - (own * MOBA_BLOCK + blk_pos)[None, :]
        s_own = s_own + rel_table[t5_bucket_2(dist)].transpose(2, 0, 1)
        s_own = jnp.where(dist >= 0, s_own, -jnp.inf)
        logits = jnp.concatenate(
            [s_past.reshape(bsz, n_heads, MOBA_QCHUNK, topk * MOBA_BLOCK), s_own], axis=-1)
        p = jax.nn.softmax(logits, axis=-1)
        p_past = p[..., :topk * MOBA_BLOCK].reshape(bsz, n_heads, MOBA_QCHUNK, topk, MOBA_BLOCK)
        p_own = p[..., topk * MOBA_BLOCK:]
        o = (jnp.einsum('bhqnk,bhqnkd->bhqd', p_past.astype(vg.dtype), vg,
                        preferred_element_type=jnp.float32)
             + jnp.einsum('bhqk,bhkd->bhqd', p_own.astype(v_own.dtype), v_own,
                          preferred_element_type=jnp.float32))
        return o.astype(q.dtype)

    out = lax.map(chunk, jnp.arange(s_pad // MOBA_QCHUNK))
    out = out.transpose(1, 0, 3, 2, 4).reshape(bsz, s_pad, n_heads * d_head)
    return out[:, :seq]

def _lru_combine(c1, c2):
    a1, b1 = c1
    a2, b2 = c2
    return a1 * a2, a2 * b1 + b2

def rg_lru_branch(xr, gate_br, conv_w, conv_b, wa, ba, wx, bx, lam):
    xc = causal_depthwise_conv(xr, conv_w) + conv_b
    bsz, seq, width = xc.shape
    xg = xc.reshape(bsz, seq, LRU_BLOCKS, LRU_BW)
    r = jax.nn.sigmoid((jnp.einsum('bsgi,gij->bsgj', xg, wa).reshape(bsz, seq, width) + ba)
                       .astype(jnp.float32))
    i = jax.nn.sigmoid((jnp.einsum('bsgi,gij->bsgj', xg, wx).reshape(bsz, seq, width) + bx)
                       .astype(jnp.float32))
    log_a = -LRU_C * r * jax.nn.softplus(-lam.astype(jnp.float32))
    a = jnp.exp(log_a)
    mult = jnp.sqrt(-jnp.expm1(2.0 * log_a))
    u = mult * i * xc.astype(jnp.float32)
    _, h = lax.associative_scan(_lru_combine, (a, u), axis=1)
    return (h * jax.nn.gelu(gate_br.astype(jnp.float32))).astype(xr.dtype)

def short_conv_branch(b, c, xs, conv_w):
    return b * causal_depthwise_conv(c * xs, conv_w)

def second_inputs(seed: int = 0) -> dict:
    key = jax.random.key(seed)
    ks = jax.random.split(key, 24)
    f32 = jnp.float32
    nrm = lambda k, shape, fan_in: jax.random.normal(k, shape, f32) * (fan_in ** -0.5)
    u = jax.random.uniform(ks[12], (DEPTH_2, LRU_W), f32, minval=0.9, maxval=0.999)
    a_base = u ** (1.0 / LRU_C)
    lam = jnp.log(a_base) - jnp.log1p(-a_base)
    return {
        "x": jax.random.normal(ks[0], (BATCH, SEQ, D_MODEL), f32),
        "norm_mix_g": 1.0 + 0.02 * jax.random.normal(ks[1], (DEPTH_2, D_MODEL), f32),
        "w_in": nrm(ks[2], (DEPTH_2, D_MODEL, N_IN), D_MODEL),
        "gate_b": 0.02 * jax.random.normal(ks[3], (DEPTH_2, N_BRANCH * D_MODEL), f32),
        "rel_table": 0.1 * jax.random.normal(ks[4], (N_BUCKETS, N_HEADS), f32),
        "w_attn_o": nrm(ks[5], (DEPTH_2, ATTN_W, D_MODEL), ATTN_W),
        "lru_conv_w": nrm(ks[6], (DEPTH_2, LRU_CONV, LRU_W), LRU_CONV),
        "lru_conv_b": 0.02 * jax.random.normal(ks[7], (DEPTH_2, LRU_W), f32),
        "lru_wa": nrm(ks[8], (DEPTH_2, LRU_BLOCKS, LRU_BW, LRU_BW), LRU_BW),
        "lru_ba": 0.02 * jax.random.normal(ks[9], (DEPTH_2, LRU_W), f32),
        "lru_wx": nrm(ks[10], (DEPTH_2, LRU_BLOCKS, LRU_BW, LRU_BW), LRU_BW),
        "lru_bx": 0.02 * jax.random.normal(ks[11], (DEPTH_2, LRU_W), f32),
        "lru_lambda": lam,
        "w_lru_o": nrm(ks[13], (DEPTH_2, LRU_W, D_MODEL), LRU_W),
        "sc_conv_w": nrm(ks[14], (DEPTH_2, SC_CONV, SC_W), SC_CONV),
        "w_sc_o": nrm(ks[15], (DEPTH_2, SC_W, D_MODEL), SC_W),
        "w_out": nrm(ks[16], (DEPTH_2, D_MODEL, D_MODEL), D_MODEL),
        "norm_mlp_g": 1.0 + 0.02 * jax.random.normal(ks[17], (DEPTH_2, D_MODEL), f32),
        "w_mlp_up": nrm(ks[18], (DEPTH_2, D_MODEL, D_FF), D_MODEL),
        "w_mlp_down": nrm(ks[19], (DEPTH_2, D_FF, D_MODEL), D_FF),
        "final_g": 1.0 + 0.02 * jax.random.normal(ks[20], (D_MODEL,), f32),
    }

def second_block(x, norm_mix_g, w_in, gate_b, rel_table, w_attn_o, lru_conv_w, lru_conv_b,
              lru_wa, lru_ba, lru_wx, lru_bx, lru_lambda, w_lru_o, sc_conv_w, w_sc_o,
              w_out, norm_mlp_g, w_mlp_up, w_mlp_down, final_g):
    bsz, seq, _ = x.shape
    offs = np.cumsum(IN_SPLITS)[:-1].tolist()
    for l in range(DEPTH_2):
        h = rms_norm_2(x, norm_mix_g[l])
        proj = h @ w_in[l]
        q, k, v, xr, gr, sc_b, sc_c, sc_x, g_pre = jnp.split(proj, offs, axis=-1)
        heads = (bsz, seq, N_HEADS, HEAD_DIM)
        y_a = moba_attention(q.reshape(heads), k.reshape(heads), v.reshape(heads),
                             rel_table) @ w_attn_o[l]
        y_b = rg_lru_branch(xr, gr, lru_conv_w[l], lru_conv_b[l], lru_wa[l], lru_ba[l],
                            lru_wx[l], lru_bx[l], lru_lambda[l]) @ w_lru_o[l]
        y_c = short_conv_branch(sc_b, sc_c, sc_x, sc_conv_w[l]) @ w_sc_o[l]
        g_a, g_b, g_c = jnp.split(jax.nn.sigmoid(g_pre + gate_b[l]), N_BRANCH, axis=-1)
        x = x + (g_a * y_a + g_b * y_b + g_c * y_c) @ w_out[l]
        h = rms_norm_2(x, norm_mlp_g[l])
        x = x + jnp.square(jax.nn.relu(h @ w_mlp_up[l])) @ w_mlp_down[l]
    return rms_norm_2(x, final_g)


def setup_inputs(seed=0):
    out = dict(first_inputs(seed))
    for name, value in second_inputs(seed + 1).items():
        if name != "x":
            out[name + "_2"] = value
    return out


def reference(
    x, rel_bias, even_norm, even_w_in, even_pool_w, even_pool_scale, even_q_gain, even_k_gain,
    even_w_out, odd_norm, odd_w_in, odd_q_gain, odd_k_gain, odd_sinks, odd_w_out, norm_mix_g_2,
    w_in_2, gate_b_2, rel_table_2, w_attn_o_2, lru_conv_w_2, lru_conv_b_2, lru_wa_2, lru_ba_2,
    lru_wx_2, lru_bx_2, lru_lambda_2, w_lru_o_2, sc_conv_w_2, w_sc_o_2, w_out_2, norm_mlp_g_2,
    w_mlp_up_2, w_mlp_down_2, final_g_2,
):
    x = first_block(
        x, rel_bias, even_norm, even_w_in, even_pool_w, even_pool_scale, even_q_gain,
        even_k_gain, even_w_out, odd_norm, odd_w_in, odd_q_gain, odd_k_gain, odd_sinks,
        odd_w_out,
    )
    return second_block(
        x, norm_mix_g_2, w_in_2, gate_b_2, rel_table_2, w_attn_o_2, lru_conv_w_2, lru_conv_b_2,
        lru_wa_2, lru_ba_2, lru_wx_2, lru_bx_2, lru_lambda_2, w_lru_o_2, sc_conv_w_2, w_sc_o_2,
        w_out_2, norm_mlp_g_2, w_mlp_up_2, w_mlp_down_2, final_g_2,
    )


_drawn_inputs = setup_inputs


def setup_inputs(seed=0):
    import zlib

    import numpy as np

    out = dict(_drawn_inputs(seed))
    spreads = {}
    factors = {'even_norm': 2.721,
     'even_pool_scale': 5.976,
     'even_q_gain': 8.0,
     'even_k_gain': 8.0,
     'odd_norm': 8.0,
     'odd_q_gain': 8.0,
     'odd_k_gain': 8.0,
     'odd_sinks': 8.775,
     'norm_mix_g_2': 12.13,
     'gate_b_2': 30.915,
     'rel_table_2': 200.0,
     'lru_ba_2': 200.0,
     'lru_bx_2': 200.0,
     'norm_mlp_g_2': 110.139,
     'final_g_2': 21.78,
     'lru_conv_b_2': 64.0,
     'lru_lambda_2': 26.472,
     'w_attn_o_2': 7.786,
     'lru_conv_w_2': 8.0,
     'lru_wa_2': 8.0,
     'lru_wx_2': 8.0,
     'w_lru_o_2': 8.0}
    for name, (base, spread) in spreads.items():
        noise = np.random.default_rng([zlib.crc32(name.encode()), seed]).standard_normal(out[name].shape)
        drawn = base * np.exp(spread * noise) if base else spread * noise
        out[name] = jnp.asarray(drawn.astype(out[name].dtype))
    for name, factor in factors.items():
        out[name] = (out[name] * factor).astype(out[name].dtype)
    return out
```

```python
import math
from contextlib import ExitStack, contextmanager

import numpy as np

import concourse.bass as bass
from concourse import mybir

F32 = mybir.dt.float32
F32R = mybir.dt.float32r
ALU = mybir.AluOpType
ACT = mybir.ActivationFunctionType
AX_X = mybir.AxisListType.X

P = 128
T = 256
D = 2048
NT = D // P
HALF = NT // 2
UNIT = HALF * T
EPS = 1e-6
NEG = -1.0e30
SUB = 1024
AHEAD = 4
BLK = 4 * P

DSA_HEADS, SWA_HEADS, MOBA_HEADS = 16, 32, 8
HD = 64
MHD = 128
TOPK = 64
TAKEN = -3.0e38
FUTURE = -1.0e38
ROWS = 384
LN1P_TERMS = 11
POOL_WINDOWS = (2, 4, 8, 16)

L1_PROJ = 1 + 10
L1_BLOCKS = L1_PROJ + 2 + 4
L2_BLOCKS = L1_BLOCKS + 9 + 4
L3_BLOCKS = L2_BLOCKS + 16
MIX_BLOCK = L3_BLOCKS + 4
POOL_SUBS = 4 + 80 + 2

SMALL = {}
N_SMALL = 0
for _name, _n in (("g_even", NT), ("g_odd", NT), ("g_mix", NT), ("g_mlp", NT), ("g_final", NT),
                  ("pool_scale", HALF), ("dsa_q", 1), ("dsa_k", 1), ("swa_q", 1), ("swa_k", 1),
                  ("gate_b", 3 * NT), ("conv_w", 4 * HALF), ("conv_b", HALF), ("ba", HALF),
                  ("bx", HALF), ("lam", HALF), ("sc_w", 3 * HALF), ("sinks", SWA_HEADS)):
    SMALL[_name] = N_SMALL
    N_SMALL += _n


class Count:

    def __init__(self, sem):
        self.sem, self.base, self.i, self.step = sem, 0, None, 0

    @property
    def value(self):
        return self.base if self.i is None else self.i * self.step + self.base

    def add(self, n=1):
        self.base += n
        return self.value


@contextmanager
def loop(eng, n, steps):
    starts = [c.base for c, _ in steps]
    with eng.Fori(0, n) as i:
        for c, step in steps:
            c.i, c.step = i, step
        yield i
    for (c, step), start in zip(steps, starts):
        assert c.base == start + step, (c.sem, c.base - start, step)
        c.base, c.i = start + n * step, None


class Attention:

    def __init__(self, heads, hd, row0):
        self.heads, self.hd, self.row0 = heads, hd, row0
        self.per = 512 // (4 * hd)
        self.units = [(g * self.per + c, qt, c == self.per - 1)
                      for g in range(heads // 4 // self.per) for qt in (1, 0) for c in range(self.per)]

    def banks(self, u):
        return [[0, 2], [1, 3]]

    def packs(self, u):
        blocks = [(h, kt) for h in range(4) for kt in range(self.units[u][1] + 1)]
        return [blocks[k:k + 4] for k in range(0, len(blocks), 4)]

    def n_banks(self, u):
        return sum(len(self.banks(v)) for v in range(u))

    def n_packs(self, u):
        return sum(len(self.packs(v)) for v in range(u))

    def n_flushes(self, u):
        return sum(last for *_, last in self.units[:u])


def index_banks(qt):
    n = 4 // (qt + 1)
    return [[h0 + 2 * m + odd for m in range(n)] for h0 in range(0, DSA_HEADS, 2 * n) for odd in range(2)]


DSA = Attention(DSA_HEADS, HD, 0)
SWA = Attention(SWA_HEADS, HD, DSA_HEADS)
MOBA = Attention(MOBA_HEADS, MHD, DSA_HEADS + SWA_HEADS)
BEFORE = {}
_u = _b = _p = _f = 0
for _a in (DSA, SWA, MOBA):
    BEFORE[_a] = (_u, _b, _p, _f)
    _n = len(_a.units)
    _u, _b, _p, _f = _u + _n, _b + _a.n_banks(_n), _p + _a.n_packs(_n), _f + _a.n_flushes(_n)


def build(nc, x_in, w_in, small_in, tables_in, onehot_in, const_in, out):
    n_subs = w_in.shape[0]
    bias_rows = nc.dram_tensor("bias_rows", [DSA_HEADS + SWA_HEADS + MOBA_HEADS, P, ROWS + 1], F32,
                               kind="Internal")
    bias_head = P * (ROWS + 1)
    place = [-(-nc.sbuf_base // 64) * 64]

    def fixed(name, shape, dt=F32):
        t = nc.alloc_sbuf_tensor_at(name, shape, dt, offset=place[0])
        place[0] += -(-4 * int(np.prod(shape[1:])) // 32) * 32
        assert place[0] <= nc.sbuf_usable_end, (name, place[0])
        return t

    def view(name, shape, offset, dt=F32):
        return nc.alloc_sbuf_tensor_at(name, shape, dt, offset=offset)

    with ExitStack() as ctx:
        def sem(name):
            return ctx.enter_context(nc.semaphore(name))

        X = fixed("X", [P, NT, T])
        RAW = fixed("RAW", [P, AHEAD, SUB])
        WH = fixed("WH", [P, AHEAD, SUB], F32R)
        WL = fixed("WL", [P, AHEAD, SUB], F32R)
        HH = fixed("HH", [P, NT, T], F32R)
        HL = fixed("HL", [P, NT, T], F32R)
        g_at = place[0]
        GH = fixed("GH", [P, NT, T], F32R)
        GL = fixed("GL", [P, NT, T], F32R)
        s_at = place[0]
        S = fixed("S", [P, 8 * HALF, T])
        small = fixed("small", [P, N_SMALL])
        ident = fixed("ident", [P, P])
        ones = fixed("ones", [P, P])
        pair = fixed("pair", [P, 2])
        rs = fixed("rs", [P, T])
        pts = fixed("pts", [P, 2, 512])
        SQACC = fixed("SQACC", [P, 2, T])
        SQTMP = fixed("SQTMP", [P, 2, T])
        TF = fixed("TF", [P, 512])
        o_sb = fixed("o_sb", [P, 512])
        rq = fixed("rq", [P, 64])
        neg_max = fixed("neg_max", [P, 4, 4])
        sums = fixed("sums", [P, 2, 8])
        r_sums = fixed("r_sums", [P, 8])
        sink_d = fixed("sink_d", [P, 4, 4])
        sink_e = fixed("sink_e", [P, 2, 8])
        gg = fixed("gg", [P, 2])

        def unit(k):
            return s_at + 4 * UNIT * k

        def gunit(k):
            return g_at + 4 * UNIT * k

        def col(name, k=0, n=1):
            a = SMALL[name] + k
            return small[:, a:a + n]

        TABS = view("TABS", [33, 96], unit(5))
        ONEHOT = view("ONEHOT", [33, 3, ROWS], unit(6))
        ROWS_SB = view("ROWS_SB", [32, 3, ROWS], unit(7))
        EA, EB, KT1, IKT = S[:, 40, :], S[:, 41, :], S[:, 42, :], S[:, 43, :]
        V1 = view("V1", [P, 2, P], unit(5) + 16 * T)
        IW = view("IW", [P, 2, P], unit(5) + 20 * T)
        SCORE = view("SCORE", [P, 384], unit(5) + 24 * T)
        TOP8 = view("TOP8", [P, 2, 8], unit(5) + 30 * T)
        INV = view("INV", [P, 4, 16], unit(5) + 30 * T + 64)
        RELU = view("RELU", [P, 2, 512], gunit(0))
        SQ1 = view("SQ1", [P, HALF, T], gunit(2))
        KSQ1 = view("KSQ1", [P, T], gunit(0) + 16 * T)
        RK1 = view("RK1", [P, T], gunit(0) + 20 * T)
        PLH = view("PLH", [P, HALF, T], unit(6), F32R)
        PLL = view("PLL", [P, HALF, T], unit(7), F32R)
        K2 = view("K2", [P, 4, T], unit(4))
        V2 = view("V2", [P, 2, 2, P], unit(4) + 16 * T)
        KV2 = view("KV2", [P, 4, T], unit(5))
        KSQ2 = view("KSQ2", [P, 2, T], unit(5) + 16 * T)
        RK2 = view("RK2", [P, 2, T], unit(5) + 24 * T)
        SQ2 = view("SQ2", [P, HALF, T], unit(7))
        V3T = view("V3T", [P, HALF, T], gunit(0))
        V3 = view("V3", [P, 2, HALF, P], gunit(3))
        SCH = view("SCH", [P, HALF, T], unit(5), F32R)
        SCL = view("SCL", [P, HALF, T], unit(6), F32R)
        XCH = view("XCH", [P, HALF, T], unit(1), F32R)
        XCL = view("XCL", [P, HALF, T], unit(4), F32R)
        LRU_A = view("LRU_A", [P, HALF, T], gunit(3))
        LRU_M = view("LRU_M", [P, HALF, T], gunit(1))
        SP8 = view("SP8", [P, 8, HALF], unit(7))
        MIX = S[:, 0:16, :]
        SG = S[:, 16:20, :]
        MT = S[:, 20:24, :]
        UT = S[:, 0:4, :]
        UU = S[:, 4:8, :]
        LBUF = {a: view(f"L{n}", [P, 2, 4, T], o) for n, (a, o) in
                enumerate(((DSA, unit(7)), (SWA, unit(5)), (MOBA, gunit(1))))}
        BBUF = {a: view(f"B{n}", [P, 2, 4, T], o) for n, (a, o) in
                enumerate(((DSA, unit(6)), (SWA, unit(6)), (MOBA, unit(7))))}

        GP = ctx.enter_context(nc.psum_tensor("GP", [P, 2, 4, T], F32))
        LOG = ctx.enter_context(nc.psum_tensor("LOG", [P, 2, 512], F32))
        PT = ctx.enter_context(nc.psum_tensor("PT", [P, 4, P], F32))
        OP = ctx.enter_context(nc.psum_tensor("OP", [P, 512], F32))

        raw_full = [sem(f"raw_full{k}") for k in range(AHEAD)]
        hi_ready, lo_ready, subs_used = sem("hi_ready"), sem("lo_ready"), sem("subs_used")
        psum_free = sem("psum_free")
        consts_in = sem("consts_in")
        x_in_sem = [sem(f"x_in{k}") for k in range(4)]
        hh_ready, hl_ready = sem("hh_ready"), sem("hl_ready")
        gh_ready, gl_ready = sem("gh_ready"), sem("gl_ready")
        sq_ready, ssq_done = sem("sq_ready"), sem("ssq_done")
        var_ready, std_ready = sem("var_ready"), sem("std_ready")
        gate_ready = sem("gate_ready")
        dve_step, pool_step, act_step = sem("dve_step"), sem("pool_step"), sem("act_step")
        consts_set = sem("consts_set")
        rows_done, rows_copied, rows_stored = sem("rows_done"), sem("rows_copied"), sem("rows_stored")
        bias_in = [sem("bias_in0"), sem("bias_in1")]
        idx_ready, idx_free, relu_used = sem("idx_ready"), sem("idx_free"), sem("relu_used")
        score_ready, score_causal = sem("score_ready"), sem("score_causal")
        log_ready, log_free = sem("log_ready"), sem("log_free")
        max_ready, p_ready = sem("max_ready"), sem("p_ready")
        pt_ready, pt_taken, pv_done = sem("pt_ready"), sem("pt_taken"), sem("pv_done")
        o_ready, ot_ready, ot_taken = sem("o_ready"), sem("ot_ready"), sem("ot_taken")
        out_ready, out_done = sem("out_ready"), sem("out_done")
        mix_ready, hidden_ready = sem("mix_ready"), sem("hidden_ready")
        once = {n: sem(n) for n in (
            "va_transposed", "va_taken", "ksq1", "ksq1_summed", "q1_squared", "q1_summed",
            "dsa_operands", "silu1", "pooled", "pooled_hi", "pooled_lo",
            "v2_transposed", "v2_taken", "ksq2", "ksq2_summed", "q2_squared0", "q2_squared1",
            "q2_summed0", "q2_summed1", "swa_operands", "silu2",
            "v3_transposed0", "v3_transposed1", "v3_transposed2", "v3_transposed3",
            "v3_taken0", "v3_taken1", "v3_taken2", "v3_taken3",
            "sc_ready", "sc_hi", "sc_lo", "xc_ready", "xc_hi", "xc_lo", "abs_lam", "exp_lam",
            "sp_ready", "decays", "a_squared", "m2_ready", "mult_ready", "gelu_ready",
            "lru_ready")}

        block = ctx.enter_context(nc.Block())

        @block.sync
        def _(sp):
            for k in range(AHEAD):
                sp.dma_start(RAW[:, k, :], w_in[k]).then_inc(raw_full[k], 16)
            with sp.Fori(1, n_subs // AHEAD) as i:
                for k in range(AHEAD):
                    sp.wait_ge(lo_ready, AHEAD * i + (k + 1 - AHEAD))
                    sp.dma_start(RAW[:, k, :], w_in[AHEAD * i + k]).then_inc(raw_full[k], 16)
            for n in range(4):
                sp.wait_ge(out_ready, n + 1)
                sp.dma_start(out[:, 4 * n:4 * n + 4, :], S[:, 16 + 4 * n:20 + 4 * n, :]).then_inc(out_done, 16)
            sp.wait_ge(out_done, 64)

        @block.tensor
        def _(pe):
            sub, blk = Count(subs_used), Count(psum_free)
            pt_free = [None]

            def three(o, wh, wl, rh, rl, start, stop):
                pe.matmul(o, wh, rh, start=start, stop=False, skip_group_check=True)
                pe.matmul(o, wh, rl, start=False, stop=False, skip_group_check=True)
                return pe.matmul(o, wl, rh, start=False, stop=stop, skip_group_check=True)

            def take_sub():
                pe.wait_ge(lo_ready, sub.value + 1)
                return sub.base % AHEAD

            def open_block():
                if blk.base >= 2:
                    pe.wait_ge(psum_free, blk.value - 1)
                blk.add()
                return GP[:, (blk.base - 1) % 2]

            def gemm(RH, RL, nkt=NT, k0=0, kts=2, n_out=4, ready=None):
                ps = open_block()
                for j in range(nkt // kts):
                    if ready is not None and (j * kts) % 4 == 0:
                        pe.wait_ge(ready[0], ready[1] + (j * kts) // 4 + 1)
                    slot = take_sub()
                    wh = WH[:, slot].rearrange("p (k n) -> p k n", k=kts)
                    wl = WL[:, slot].rearrange("p (k n) -> p k n", k=kts)
                    for k in range(kts):
                        kt = j * kts + k
                        for n in range(n_out):
                            c = slice(n * P, (n + 1) * P)
                            mm = three(ps[:, n], wh[:, k, c], wl[:, k, c], RH[:, k0 + kt], RL[:, k0 + kt],
                                       start=(kt == 0 and n % 2 == 0), stop=(kt == nkt - 1))
                    mm.then_inc(subs_used, 1)
                    sub.add()

            def gemms(n, RH, RL):
                with loop(pe, n, [(sub, 4 * AHEAD), (blk, 2)]):
                    for _ in range(2):
                        gemm(RH, RL)

            def ssq(n):
                pe.wait_ge(sq_ready, n + 1)
                pe.matmul(OP[:, 0:T], ones[:, :], SQACC[:, 0, :], start=True, stop=False)
                pe.matmul(OP[:, 0:T], ones[:, :], SQACC[:, 1, :], start=False, stop=True)\
                  .then_inc(ssq_done, 1)

            def transposes(src, wait, done, free):
                pe.wait_ge(*wait)
                if pt_free[0]:
                    pe.wait_ge(*pt_free[0])
                for b, ap in enumerate(src):
                    mm = pe.transpose(PT[:, b, :], ap, ident[:, :])
                mm.then_inc(done, 1)
                pt_free[0] = free

            def attend(a, q_of, k_of, v_of):
                u0, bank, pk, fl = BEFORE[a]
                L = LBUF[a]
                for u in range(len(a.units) + 1):
                    if u < len(a.units):
                        chunk, qt, _ = a.units[u]
                        nk = P * (qt + 1)
                        for heads in a.banks(u):
                            if bank >= 2:
                                pe.wait_ge(log_free, bank - 1)
                            for m, h in enumerate(heads):
                                mm = pe.matmul(LOG[:, bank % 2, m * nk:(m + 1) * nk],
                                               q_of(4 * chunk + h, qt), k_of(4 * chunk + h, nk),
                                               start=True, stop=True, skip_group_check=True)
                            mm.then_inc(log_ready, 1)
                            bank += 1
                    if u == 0:
                        continue
                    chunk, qt, last = a.units[u - 1]
                    packs, pk0 = a.packs(u - 1), pk

                    def times_v(k):
                        pe.wait_ge(pt_taken, pk0 + k + 1)
                        if k == 0 and chunk % a.per == 0 and fl:
                            pe.wait_ge(o_ready, fl)
                        for b, (h, kt) in enumerate(packs[k]):
                            c = (4 * (chunk % a.per) + h) * a.hd
                            mm = pe.matmul(OP[:, c:c + a.hd], pts[:, (pk0 + k) % 2, b * P:(b + 1) * P],
                                           v_of(4 * chunk + h, kt), start=(c == 0 and kt == 0),
                                           stop=(kt == qt), skip_group_check=True)
                        mm.then_inc(pv_done, 1)

                    for k, blocks in enumerate(packs):
                        transposes([L[:, (u - 1) % 2, h, kt * P:(kt + 1) * P] for h, kt in blocks],
                                   (p_ready, u0 + u), pt_ready, (pt_taken, pk + 1))
                        pk += 1
                        if k:
                            times_v(k - 1)
                    times_v(len(packs) - 1)
                    if last:
                        fl += 1
                        transposes([o_sb[:, b * P:(b + 1) * P] for b in range(4)],
                                   (o_ready, fl), ot_ready, (ot_taken, fl))

            pe.wait_ge(consts_in, 16 * 5)
            for k, o in enumerate((LOG[0:32, 0, 0:ROWS], LOG[0:32, 1, 0:ROWS], OP[0:32, 0:ROWS])):
                mm = pe.matmul(o, TABS[0:33, 32 * k:32 * k + 32], ONEHOT[0:33, k, :], start=True, stop=True)
            mm.then_inc(rows_done, 1)

            gemm(HH, HL, kts=4, n_out=2, ready=(hl_ready, 0))
            pe.wait_ge(rows_copied, 1)
            pe.wait_ge(consts_set, 1)
            ssq(0)
            gemms(5, HH, HL)
            transposes([(EA, EB)[b // 2][:, (b % 2) * P:(b % 2 + 1) * P] for b in range(4)],
                       (psum_free, 1), once["va_transposed"], (once["va_taken"], 1))
            pe.wait_ge(once["ksq1"], 1)
            pe.matmul(LOG[:, 0, 0:T], ones[0:HD, :], KSQ1[0:HD, :], start=True, stop=True)\
              .then_inc(once["ksq1_summed"], 1)
            pe.wait_ge(once["q1_squared"], 1)
            for qt in range(2):
                for t in range(HALF):
                    c = DSA_HEADS * qt + 2 * t
                    mm = pe.matmul(LOG[:, 1, c:c + 2], SQ1[:, t, qt * P:(qt + 1) * P], pair[:, :],
                                   start=True, stop=True, skip_group_check=True)
            mm.then_inc(once["q1_summed"], 1)
            pe.wait_ge(once["q1_summed"], 1)
            pe.wait_ge(std_ready, 3)
            n = 0
            for qt in (1, 0):
                nk = P * (qt + 1)
                for heads in index_banks(qt):
                    if n >= 2:
                        pe.wait_ge(idx_free, n - 1)
                    for m, h in enumerate(heads):
                        r = slice(HD * (h % 2), HD * (h % 2) + HD)
                        mm = pe.matmul(LOG[:, n % 2, m * nk:(m + 1) * nk],
                                       S[r, h // 2, qt * P:(qt + 1) * P], IKT[r, 0:nk],
                                       start=True, stop=True, skip_group_check=True)
                    mm.then_inc(idx_ready, 1)
                    n += 1
            pe.wait_ge(idx_free, n)
            pe.wait_ge(once["dsa_operands"], 1)

            def half_rows(tile_of):
                return lambda h, qt: S[HD * (h % 2):HD * (h % 2) + HD, tile_of(h), qt * P:(qt + 1) * P]

            attend(DSA, half_rows(lambda h: HALF + h // 2),
                   lambda h, nk: KT1[HD * (h % 2):HD * (h % 2) + HD, 0:nk],
                   lambda h, kt: V1[:, kt, HD:2 * HD])
            for half in range(2):
                ps = open_block()
                pe.wait_ge(once["pooled_lo"], 1)
                slot = take_sub()
                wh = WH[:, slot].rearrange("p (g k n) -> p g k n", g=2, k=2)
                wl = WL[:, slot].rearrange("p (g k n) -> p g k n", g=2, k=2)
                for g in range(2):
                    for k in range(2):
                        for n in range(2):
                            c = slice(n * P, (n + 1) * P)
                            kt = 4 * half + 2 * g + k
                            mm = three(ps[:, 2 * g + n], wh[:, g, k, c], wl[:, g, k, c], PLH[:, kt], PLL[:, kt],
                                       start=(k == 0 and n == 0), stop=(k == 1))
                mm.then_inc(subs_used, 1)
                sub.add()
            pe.wait_ge(gl_ready, 6)
            gemms(2, GH, GL)

            gemm(HH, HL, ready=(hl_ready, 4))
            ssq(1)
            gemms(4, HH, HL)
            transposes([KV2[:, 2 + b % 2, (b // 2) * P:(b // 2 + 1) * P] for b in range(4)],
                       (psum_free, L1_BLOCKS + 1), once["v2_transposed"], (once["v2_taken"], 1))
            pe.wait_ge(once["ksq2"], 1)
            for a in range(2):
                r = slice(HD * a, HD * a + HD)
                mm = pe.matmul(LOG[r, 0, :].rearrange("p (a t) -> p a t", a=2), ones[r, 0:HD], KSQ2[r, :, :],
                               start=True, stop=True, skip_group_check=True)
            mm.then_inc(once["ksq2_summed"], 1)
            for part in range(2):
                pe.wait_ge(once[f"q2_squared{part}"], 1)
                for qt in range(2):
                    for t in range(HALF):
                        c = SWA_HEADS * qt + NT * part + 2 * t
                        mm = pe.matmul(LOG[:, 1, c:c + 2], SQ2[:, t, qt * P:(qt + 1) * P], pair[:, :],
                                       start=True, stop=True, skip_group_check=True)
                mm.then_inc(once[f"q2_summed{part}"], 1)
            pe.wait_ge(once["swa_operands"], 1)
            attend(SWA, half_rows(lambda h: h // 2),
                   lambda h, nk: K2[HD * (h % 2):HD * (h % 2) + HD, h // 8, 0:nk],
                   lambda h, kt: V2[:, kt, h // 16, HD * (h // 8 % 2):HD * (h // 8 % 2) + HD])
            pe.wait_ge(gl_ready, 14)
            gemms(2, GH, GL)

            for b in range(2):
                gemm(HH, HL, ready=(hl_ready, 8))
                if b == 0:
                    ssq(2)
            gemms(7, HH, HL)
            for b in range(2):
                for kt in range(2):
                    k = 2 * b + kt
                    transposes([V3T[:, 4 * b + t, kt * P:(kt + 1) * P] for t in range(4)],
                               (psum_free, L2_BLOCKS + 1 + b), once[f"v3_transposed{k}"],
                               (once[f"v3_taken{k}"], 1))
            pe.wait_ge(psum_free, L3_BLOCKS)
            attend(MOBA, lambda h, qt: S[:, h, qt * P:(qt + 1) * P], lambda h, nk: S[:, HALF + h, 0:nk],
                   lambda h, kt: V3[:, kt, h, :])
            pe.wait_ge(once["xc_lo"], 1)
            for half in range(2):
                slot = take_sub()
                for gate in range(2):
                    ps = open_block()
                    for n in range(4):
                        c = slice((4 * gate + n) * P, (4 * gate + n + 1) * P)
                        mm = three(ps[:, n], WH[:, slot, c], WL[:, slot, c], XCH[:, 4 * half + n],
                                   XCL[:, 4 * half + n], start=(n % 2 == 0), stop=True)
                mm.then_inc(subs_used, 1)
                sub.add()
            pe.wait_ge(gl_ready, 19)
            pe.wait_ge(once["sc_lo"], 1)
            for BH, BL, k0 in ((GH, GL, 0), (GH, GL, HALF), (SCH, SCL, 0)):
                with loop(pe, 2, [(sub, 6 * AHEAD), (blk, 4)]):
                    for _ in range(2):
                        gemm(HH, HL)
                        gemm(BH, BL, nkt=HALF, k0=k0)
            gemm(GH, GL, ready=(gl_ready, 19))
            gemm(GH, GL)
            gemms(1, GH, GL)

            gemm(HH, HL, ready=(hl_ready, 12))
            ssq(3)
            gemm(HH, HL)
            gemms(1, HH, HL)
            for g in range(4):
                if g:
                    gemms(2, HH, HL)
                gemm(GH, GL, ready=(gl_ready, 23 + 4 * g))
                gemm(GH, GL)
                gemms(1, GH, GL)
            ssq(4)

        @block.scalar
        def _(act):
            sub, blk = Count(hi_ready), Count(psum_free)
            raw = [Count(raw_full[k]) for k in range(AHEAD)]
            gr, var, mix, hidden = Count(gate_ready), Count(var_ready), Count(mix_ready), Count(hidden_ready)
            rounds = [(sub, 16), (blk, 2)] + [(c, 16 * 4) for c in raw]

            def splits(n):
                for _ in range(n):
                    slot = sub.base % AHEAD
                    act.wait_ge(raw_full[slot], raw[slot].add(16))
                    if sub.i is not None or sub.base >= AHEAD:
                        act.wait_ge(subs_used, sub.value - (AHEAD - 1))
                    act.activation(WH[:, slot], RAW[:, slot], ACT.Copy).then_inc(hi_ready, 1)
                    sub.add()

            def block_splits():
                splits(8)
                blk.add()

            def root(src, dst):
                act.wait_ge(var_ready, var.add())
                act.activation(dst, src, ACT.Sqrt).then_inc(std_ready, 1)

            def token_root():
                root(TF[:, 0:T], TF[:, T:])

            def h_hi(gain, t0, ready):
                act.wait_ge(*ready)
                for k in range(4):
                    ins = act.activation(HH[:, bass.ds(t0 + k, 1), :], X[:, bass.ds(t0 + k, 1), :], ACT.Copy,
                                         scale=small[:, bass.ds(t0 + (SMALL[gain] + k), 1)])
                ins.then_inc(hh_ready, 1)

            def residual_blocks(gain):
                with loop(act, 2, rounds) as i:
                    for b in range(2):
                        block_splits()
                        h_hi(gain, 8 * i + 4 * b, (psum_free, blk.value))

            def attend(a):
                u0, _, pk, fl = BEFORE[a]
                L = LBUF[a]
                for u in range(len(a.units) + 1):
                    if u:
                        for _ in a.packs(u - 1):
                            act.wait_ge(pt_ready, pk + 1)
                            if pk >= 2:
                                act.wait_ge(pv_done, pk - 1)
                            act.activation(pts[:, pk % 2, :].rearrange("p (b q) -> p b q", b=4), PT[:, :, :],
                                           ACT.Copy).then_inc(pt_taken, 1)
                            pk += 1
                    if u < len(a.units):
                        chunk, qt, _ = a.units[u]
                        nk = P * (qt + 1)
                        act.wait_ge(max_ready, u0 + u + 1)
                        f = BEFORE[a][3] + a.n_flushes(u)
                        c = 4 * (chunk % a.per)
                        if a is SWA:
                            act.activation(sink_e[:, f % 2, c:c + 4], sink_d[:, u % 4, :], ACT.Exp)
                        for h in range(4):
                            ins = act.activation(L[:, u % 2, h, 0:nk], L[:, u % 2, h, 0:nk], ACT.Exp,
                                                 bias=neg_max[:, u % 4, h:h + 1],
                                                 accum_out=sums[:, f % 2, c + h:c + h + 1])
                        ins.then_inc(p_ready, 1)
                    if u and a.units[u - 1][2]:
                        qt = a.units[u - 1][1]
                        t0 = 4 * (a.n_flushes(u - 1) // 2) + (HALF if a is DSA else 0)
                        fl += 1
                        act.wait_ge(ot_taken, fl)
                        act.activation(GH[:, t0:t0 + 4, qt * P:(qt + 1) * P],
                                       TF[:, :].rearrange("p (b q) -> p b q", b=4), ACT.Copy).then_inc(gh_ready, 1)

            for n in range(4):
                act.dma_start(X[:, 4 * n:4 * n + 4, :], x_in[:, 4 * n:4 * n + 4, :]).then_inc(x_in_sem[n], 16)
            act.dma_start(small[:, :], small_in).then_inc(consts_in, 16)
            act.dma_start(TABS[:, :], tables_in).then_inc(consts_in, 16)
            act.dma_start(ONEHOT[:, :, :], onehot_in).then_inc(consts_in, 16)
            act.dma_start(ident[:, :], const_in[:, 0:P]).then_inc(consts_in, 16)
            act.dma_start(INV[:, :, :], const_in[:, P:P + 64].rearrange("p (g t) -> p g t", g=4))\
               .then_inc(consts_in, 16)
            splits(2)
            act.wait_ge(consts_in, 16 * 5)
            for n in range(4):
                h_hi("g_even", 4 * n, (x_in_sem[n], 16))
            splits(2)

            splits(4)
            blk.add()
            token_root()
            with loop(act, 5, rounds):
                for _ in range(2):
                    block_splits()
            act.wait_ge(psum_free, blk.value)
            act.activation(KSQ1[0:HD, :], EA[0:HD, :], ACT.Square).then_inc(once["ksq1"], 1)
            act.activation(SQ1[:, :, :], S[:, HALF:2 * HALF, :], ACT.Square).then_inc(once["q1_squared"], 1)
            root(TF[:, 0:T], TF[:, T:])
            root(TF[:, 0:32], TF[:, T:T + 32])
            act.activation(S[:, 16:24, :], S[:, 16:24, :], ACT.Silu)
            act.activation(S[:, 32:40, :], S[:, 32:40, :], ACT.Silu).then_inc(once["silu1"], 1)
            for n in range(12):
                act.wait_ge(idx_ready, n + 1)
                if n >= 2:
                    act.wait_ge(relu_used, n - 1)
                act.activation(RELU[:, n % 2, :], LOG[:, n % 2, :], ACT.Relu).then_inc(idx_free, 1)
            attend(DSA)
            act.wait_ge(once["pooled"], 1)
            act.activation(PLH[:, :, :], S[:, 16:24, :], ACT.Copy).then_inc(once["pooled_hi"], 1)
            for half in range(2):
                splits(1)
                blk.add()
                act.wait_ge(psum_free, blk.value)
                act.activation(GH[:, 4 * half:4 * half + 4, :], S[:, 24 + 4 * half:28 + 4 * half, :], ACT.Copy)\
                   .then_inc(gh_ready, 1)
            residual_blocks("g_odd")

            block_splits()
            token_root()
            with loop(act, 4, rounds):
                for _ in range(2):
                    block_splits()
            act.wait_ge(psum_free, blk.value)
            act.activation(KSQ2[:, :, :], KV2[:, 0:2, :], ACT.Square).then_inc(once["ksq2"], 1)
            for part in range(2):
                if part:
                    act.wait_ge(once["q2_summed0"], 1)
                act.activation(SQ2[:, :, :], S[:, HALF * part:HALF * part + HALF, :], ACT.Square)\
                   .then_inc(once[f"q2_squared{part}"], 1)
            root(TF[:, :].rearrange("p (a t) -> p a t", a=2), o_sb[:, :].rearrange("p (a t) -> p a t", a=2))
            root(TF[:, 0:64], TF[:, T:T + 64])
            act.activation(S[:, 16:32, :], S[:, 16:32, :], ACT.Silu).then_inc(once["silu2"], 1)
            attend(SWA)
            residual_blocks("g_mix")

            block_splits()
            token_root()
            block_splits()
            with loop(act, 7, rounds):
                for _ in range(2):
                    block_splits()
            attend(MOBA)
            act.wait_ge(once["sc_ready"], 1)
            act.activation(SCH[:, :, :], S[:, 48:56, :], ACT.Copy).then_inc(once["sc_hi"], 1)
            act.wait_ge(once["xc_ready"], 1)
            act.activation(XCH[:, :, :], S[:, 0:8, :], ACT.Copy).then_inc(once["xc_hi"], 1)
            act.wait_ge(once["abs_lam"], 1)
            act.activation(SP8[:, 1, :], SP8[:, 0, :], ACT.Exp, scale=-1.0).then_inc(once["exp_lam"], 1)
            act.activation(S[:, 24:32, :], S[:, 24:32, :], ACT.Gelu_apprx_tanh).then_inc(once["gelu_ready"], 1)
            for half in range(2):
                splits(1)
                act.wait_ge(subs_used, sub.base - AHEAD)
                for gate, (dst, b) in enumerate(((LRU_M[:, :, :], "ba"), (S[:, 16:24, :], "bx"))):
                    for n in range(4):
                        t = 4 * half + n
                        ins = act.activation(dst[:, t, :], GP[:, gate, n, :], ACT.Sigmoid, bias=col(b, t))
                    ins.then_inc(psum_free, 1)
                    blk.add()
            act.wait_ge(psum_free, blk.value)
            act.wait_ge(once["sp_ready"], 1)
            for t in range(HALF):
                ins = act.activation(LRU_A[:, t, :], LRU_M[:, t, :], ACT.Exp, scale=SP8[:, 6, t:t + 1])
            ins.then_inc(once["decays"], 1)
            act.wait_ge(once["decays"], 1)
            for t in range(HALF):
                act.activation(LRU_M[:, t, :], LRU_M[:, t, :], ACT.Tanh, scale=SP8[:, 7, t:t + 1])
            act.activation(S[:, 8:16, :], LRU_A[:, :, :], ACT.Square).then_inc(once["a_squared"], 1)
            act.wait_ge(once["m2_ready"], 1)
            act.activation(LRU_M[:, :, :], LRU_M[:, :, :], ACT.Sqrt, scale=2.0 ** 100)\
               .then_inc(once["mult_ready"], 1)
            act.wait_ge(once["lru_ready"], 1)
            act.activation(GH[:, 8:16, :], S[:, 24:32, :], ACT.Copy).then_inc(gh_ready, 1)
            for branch in range(3):
                last = branch == 2
                steps = [(sub, 24), (blk, 4)] + [(c, 16 * 6) for c in raw] + [(mix, 2)] * last
                with loop(act, 2, steps) as i:
                    for b in range(2):
                        block_splits()
                        act.wait_ge(psum_free, blk.value)
                        for k in range(4):
                            t = 8 * i + (4 * b + k + SMALL["gate_b"] + NT * branch)
                            ins = act.activation(SG[:, k, :], MT[:, k, :], ACT.Sigmoid,
                                                 bias=small[:, bass.ds(t, 1)])
                        ins.then_inc(gate_ready, 1)
                        splits(4)
                        blk.add()
                        if last:
                            t = bass.ds(8 * i + 4 * b, 4)
                            act.wait_ge(mix_ready, mix.add())
                            act.activation(GH[:, t, :], MIX[:, t, :], ACT.Copy).then_inc(gh_ready, 1)
            residual_blocks("g_mlp")

            def hidden_hi(t0):
                act.wait_ge(hidden_ready, hidden.add())
                act.activation(GH[:, bass.ds(t0, 4), :], UU, ACT.Copy).then_inc(gh_ready, 1)

            for g in range(4):
                if g == 0:
                    block_splits()
                    token_root()
                    hidden_hi(0)
                    for b in range(1, 4):
                        block_splits()
                        hidden_hi(4 * b)
                else:
                    with loop(act, 2, rounds + [(hidden, 2)]) as i:
                        for b in range(2):
                            block_splits()
                            hidden_hi(8 * i + 4 * b)
                if g < 3:
                    with loop(act, 2, rounds):
                        for _ in range(2):
                            block_splits()
            splits(n_subs - sub.base)
            token_root()

        @block.vector
        def _(dve):
            sub, used, blk = Count(lo_ready), Count(subs_used), Count(psum_free)
            hh, gh, gr, steps_n = Count(hh_ready), Count(gh_ready), Count(gate_ready), Count(dve_step)
            std = Count(std_ready)
            rounds = [(sub, 16), (used, 16), (blk, 2)]

            def splits(n):
                for _ in range(n):
                    slot = sub.base % AHEAD
                    dve.wait_ge(hi_ready, sub.value + 1)
                    dve.tensor_tensor(WL[:, slot], RAW[:, slot], WH[:, slot].bitcast(F32), ALU.subtract)\
                       .then_inc(lo_ready, 1)
                    sub.add()

            def step(ins):
                ins.then_inc(dve_step, 1)
                dve.wait_ge(dve_step, steps_n.add())

            def block_done(n=8):
                dve.wait_ge(subs_used, used.add(n))
                blk.add()
                return GP[:, (blk.base - 1) % 2]

            def rs_of(n):
                return rs[:, None, :].to_broadcast([P, n, T])

            def times_rs(dst):
                ps = block_done()
                for k in (0, 2):
                    ins = dve.tensor_tensor(dst(k), ps[:, k:k + 2], rs_of(2), ALU.mult)
                ins.then_inc(psum_free, 1)

            def rsqrt(src, n, var, tmp, y, ready):
                dve.wait_ge(*ready)
                dve.tensor_scalar(var, src, 1.0 / n, EPS, ALU.mult, ALU.add).then_inc(var_ready, 1)
                dve.wait_ge(std_ready, std.add())
                step(dve.reciprocal(y, tmp))
                step(dve.tensor_tensor(tmp, y, y, ALU.mult))
                step(dve.tensor_tensor(tmp, tmp, var, ALU.mult))
                step(dve.tensor_scalar(tmp, tmp, -0.5, 1.5, ALU.mult, ALU.add))
                step(dve.tensor_tensor(y, y, tmp, ALU.mult))

            def token_norm(n):
                rsqrt(OP[:, 0:T], D, TF[:, 0:T], TF[:, T:], rs[:, :], (ssq_done, n + 1))

            def h_lo(gain, t0):
                dve.wait_ge(hh_ready, hh.add())
                for k in range(4):
                    s = bass.ds(t0 + k, 1)
                    ins = dve.scalar_tensor_tensor(out=HL[:, s, :], in0=X[:, s, :],
                                                   scalar=small[:, bass.ds(t0 + (SMALL[gain] + k), 1)],
                                                   in1=HH[:, s, :].bitcast(F32), op0=ALU.mult, op1=ALU.subtract)
                ins.then_inc(hl_ready, 1)

            def g_lo(dst, src, hi):
                dve.wait_ge(gh_ready, gh.add())
                dve.tensor_tensor(dst, src, hi.bitcast(F32), ALU.subtract).then_inc(gl_ready, 1)

            def add_residual(t0):
                ps = block_done()
                for k in (0, 2):
                    s = bass.ds(t0 + k, 2)
                    ins = dve.tensor_tensor(X[:, s, :], ps[:, k:k + 2], X[:, s, :], ALU.add)
                ins.then_inc(psum_free, 1)

            def residual_blocks(gain):
                with loop(dve, 2, rounds + [(hh, 2)]) as i:
                    for b in range(2):
                        splits(8)
                        add_residual(8 * i + 4 * b)
                        h_lo(gain, 8 * i + 4 * b)

            def attend(a, scale, gate=True, mask=None):
                u0, bank, pk, fl = BEFORE[a]
                L, B = LBUF[a], BBUF[a]
                for u in range(len(a.units) + 1):
                    if u < len(a.units):
                        chunk, qt, _ = a.units[u]
                        nk, gc = P * (qt + 1), a.row0 // 4 + chunk
                        if qt:
                            dve.wait_ge(bias_in[gc % 2], 16 * (gc // 2 + 1))
                        if u >= 2:
                            dve.wait_ge(pt_ready, pk + a.n_packs(u - 1))
                        for heads in a.banks(u):
                            dve.wait_ge(log_ready, bank + 1)
                            for m, h in enumerate(heads):
                                ins = dve.scalar_tensor_tensor(
                                    out=L[:, u % 2, h, 0:nk], in0=LOG[:, bank % 2, m * nk:(m + 1) * nk],
                                    scalar=scale(4 * chunk + h, qt), in1=B[:, gc % 2, h, T - nk:T],
                                    op0=ALU.mult, op1=ALU.add)
                            ins.then_inc(log_free, 1)
                            bank += 1
                        dve.wait_ge(log_free, bank)
                        if mask is not None:
                            step(dve.tensor_tensor(L[:, u % 2, :, 0:nk], L[:, u % 2, :, 0:nk],
                                                   mask(qt)[:, None, :].to_broadcast([P, 4, nk]), ALU.add))
                        nm = neg_max[:, u % 4, :]
                        ins = dve.tensor_reduce(nm, L[:, u % 2, :, 0:nk], AX_X, ALU.max, negate=True)
                        if a is SWA:
                            step(ins)
                            sink = col("sinks", 4 * chunk, 4)
                            step(dve.scalar_tensor_tensor(out=nm, in0=sink, scalar=-1.0, in1=nm,
                                                          op0=ALU.mult, op1=ALU.min))
                            ins = dve.tensor_tensor(sink_d[:, u % 4, :], sink, nm, ALU.add)
                        ins.then_inc(max_ready, 1)
                    if u and a.units[u - 1][2]:
                        qt = a.units[u - 1][1]
                        n, g = 4 * a.per, (fl - BEFORE[a][3]) // 2
                        dve.wait_ge(p_ready, u0 + u)
                        if a is SWA:
                            step(dve.tensor_tensor(sums[:, fl % 2, 0:n], sums[:, fl % 2, 0:n],
                                                   sink_e[:, fl % 2, 0:n], ALU.add))
                        step(dve.reciprocal(r_sums[:, 0:n], sums[:, fl % 2, 0:n]))
                        dve.wait_ge(pv_done, pk + a.n_packs(u))
                        if fl:
                            dve.wait_ge(ot_ready, fl)
                        dve.tensor_tensor(o_sb[:, :].rearrange("p (h d) -> p h d", h=n),
                                          OP[:, :].rearrange("p (h d) -> p h d", h=n),
                                          r_sums[:, 0:n, None].to_broadcast([P, n, a.hd]), ALU.mult)\
                           .then_inc(o_ready, 1)
                        fl += 1
                        dve.wait_ge(ot_ready, fl)
                        tf = TF[:, :].rearrange("p (b q) -> p b q", b=4)
                        q = slice(qt * P, (qt + 1) * P)
                        if gate:
                            ins = dve.tensor_tensor(tf, PT[:, :, :], S[:, 16 + 4 * g:20 + 4 * g, q], ALU.mult)
                        else:
                            ins = dve.tensor_copy(tf, PT[:, :, :])
                        ins.then_inc(ot_taken, 1)
                        t0 = 4 * g + (HALF if a is DSA else 0)
                        g_lo(GL[:, t0:t0 + 4, q], tf, GH[:, t0:t0 + 4, q])

            splits(2)
            dve.wait_ge(consts_in, 16 * 5)
            for n in range(4):
                h_lo("g_even", 4 * n)
            dve.wait_ge(rows_done, 1)
            dve.tensor_copy(ROWS_SB[:, 0:2, :], LOG[0:32, :, 0:ROWS])
            dve.tensor_copy(ROWS_SB[:, 2, :], OP[0:32, 0:ROWS]).then_inc(rows_copied, 1)
            splits(2)
            dve.tensor_tensor(gg[:, 0:1], col("dsa_q"), col("dsa_k"), ALU.mult)
            step(dve.tensor_tensor(gg[:, 1:2], col("swa_q"), col("swa_k"), ALU.mult))

            splits(4)
            token_norm(0)
            ps = block_done(4)
            dve.tensor_tensor(S[:, 40:42, :], ps[:, 0:2], rs_of(2), ALU.mult)
            for a in range(2):
                ins = dve.tensor_tensor(IKT[HD * a:HD * a + HD, :], ps[0:HD, 1], rs[0:HD, :], ALU.mult)
            ins.then_inc(psum_free, 1)
            with loop(dve, 5, rounds) as i:
                for b in range(2):
                    splits(8)
                    times_rs(lambda k: S[:, bass.ds(8 * i + (4 * b + k), 2), :])
            dve.wait_ge(once["va_transposed"], 1)
            dve.tensor_copy(V1[:, :, :], PT[:, 0:2, :])
            dve.tensor_scalar(IW[:, :, :], PT[:, 2:4, :], DSA_HEADS ** -0.5 * HD ** -0.5, None, ALU.mult)\
               .then_inc(once["va_taken"], 1)
            rsqrt(LOG[:, 0, 0:T], HD, TF[:, 0:T], TF[:, T:], RK1[:, :], (once["ksq1_summed"], 1))
            for a in range(2):
                ins = dve.scalar_tensor_tensor(out=KT1[HD * a:HD * a + HD, :], in0=EA[0:HD, :],
                                               scalar=gg[0:HD, 0:1], in1=RK1[0:HD, :], op0=ALU.mult,
                                               op1=ALU.mult)
            step(ins)
            rsqrt(LOG[:, 1, 0:32], HD, TF[:, 0:32], TF[:, T:T + 32], rq[:, 0:32], (once["q1_summed"], 1))
            step(dve.tensor_scalar(rq[:, 0:32], rq[:, 0:32], HD ** -0.5, None, ALU.mult))
            n = 0
            dve.wait_ge(once["va_taken"], 1)
            for qt, at in ((1, 0), (0, T)):
                nk = P * (qt + 1)
                score = SCORE[:, at:at + nk]
                for heads in index_banks(qt):
                    dve.wait_ge(idx_free, n + 1)
                    for m, h in enumerate(heads):
                        w = IW[:, qt, HD + h:HD + h + 1]
                        relu = RELU[:, n % 2, m * nk:(m + 1) * nk]
                        if h == 0:
                            step(dve.tensor_scalar(score, relu, w, None, ALU.mult))
                        else:
                            step(dve.scalar_tensor_tensor(out=score, in0=relu, scalar=w, in1=score,
                                                          op0=ALU.mult, op1=ALU.add))
                    dve.sem_inc(relu_used, 1)
                    n += 1
            dve.sem_inc(score_ready, 1)
            dve.wait_ge(score_causal, 1)
            for _ in range(TOPK // 8):
                for qt, at in ((1, 0), (0, T)):
                    score = SCORE[:, at:at + P * (qt + 1)]
                    top = TOP8[:, qt, :]
                    step(dve.max(top, score))
                    step(dve.match_replace(score, top, score, TAKEN))
            step(dve.tensor_scalar(SCORE[:, :], SCORE[:, :], 0.5 * (TAKEN + FUTURE), NEG, ALU.is_gt, ALU.mult))
            dve.sem_inc(once["dsa_operands"], 1)
            dve.wait_ge(once["silu1"], 1)
            attend(DSA, lambda h, qt: rq[:, 16 * qt + h:16 * qt + h + 1],
                   mask=lambda qt: SCORE[:, 0:T] if qt else SCORE[:, T:])
            width, src = 1, S[:, 24:32, :]
            for g, w in enumerate(POOL_WINDOWS):
                dst = S[:, 8 * (g % 2):8 * (g % 2) + 8, :]
                t = slice(2 * g, HALF)
                dve.tensor_copy(dst[:, t, 0:width], src[:, t, 0:width])
                step(dve.tensor_tensor(dst[:, t, width:], src[:, t, width:], src[:, t, 0:T - width], ALU.add))
                t = slice(2 * g, 2 * g + 2)
                pin, pooled = S[:, 24 + 2 * g:26 + 2 * g, :], S[:, 16 + 2 * g:18 + 2 * g, :]
                dve.scalar_tensor_tensor(out=pooled[:, :, 16:], in0=dst[:, t, 16:], scalar=1.0 / w,
                                         in1=pin[:, :, 16:], op0=ALU.mult, op1=ALU.subtract)
                step(dve.tensor_tensor(pooled[:, :, 0:16], dst[:, t, 0:16],
                                       INV[:, g:g + 1, :].to_broadcast([P, 2, 16]), ALU.mult))
                step(dve.tensor_tensor(pooled[:, :, 0:16], pooled[:, :, 0:16], pin[:, :, 0:16], ALU.subtract))
                width, src = w, dst
            dve.sem_inc(once["pooled"], 1)
            dve.wait_ge(once["pooled_hi"], 1)
            dve.tensor_tensor(PLL[:, :, :], S[:, 16:24, :], PLH[:, :, :].bitcast(F32), ALU.subtract)\
               .then_inc(once["pooled_lo"], 1)
            for half in range(2):
                splits(1)
                ps = block_done(1)
                for k in range(4):
                    t = 4 * half + k
                    ins = dve.scalar_tensor_tensor(out=S[:, 24 + t, :], in0=ps[:, k], scalar=col("pool_scale", t),
                                                   in1=S[:, 32 + t, :], op0=ALU.mult, op1=ALU.mult)
                ins.then_inc(psum_free, 1)
                t = slice(4 * half, 4 * half + 4)
                g_lo(GL[:, t, :], S[:, 24 + 4 * half:28 + 4 * half, :], GH[:, t, :])
            residual_blocks("g_odd")

            splits(8)
            token_norm(1)
            times_rs(lambda k: KV2[:, k:k + 2, :])
            with loop(dve, 4, rounds) as i:
                for b in range(2):
                    splits(8)
                    times_rs(lambda k: S[:, bass.ds(8 * i + (4 * b + k), 2), :])
            dve.wait_ge(once["v2_transposed"], 1)
            dve.tensor_copy(V2[:, :, :, :].rearrange("p a b c -> p (a b) c"), PT[:, :, :])\
               .then_inc(once["v2_taken"], 1)
            rsqrt(LOG[:, 0, :].rearrange("p (a t) -> p a t", a=2), HD, TF[:, :].rearrange("p (a t) -> p a t", a=2),
                  o_sb[:, :].rearrange("p (a t) -> p a t", a=2), RK2[:, :, :], (once["ksq2_summed"], 1))
            for j in range(4):
                r = slice(HD * (j % 2), HD * (j % 2) + HD)
                for a in range(2):
                    ins = dve.scalar_tensor_tensor(out=K2[HD * a:HD * a + HD, j, :], in0=KV2[r, j // 2, :],
                                                   scalar=gg[r, 1:2], in1=RK2[r, j // 2, :], op0=ALU.mult,
                                                   op1=ALU.mult)
                    step(ins)
            dve.wait_ge(once["q2_summed0"], 1)
            rsqrt(LOG[:, 1, 0:64], HD, TF[:, 0:64], TF[:, T:T + 64], rq[:, :], (once["q2_summed1"], 1))
            step(dve.tensor_scalar(rq[:, :], rq[:, :], HD ** -0.5, None, ALU.mult))
            dve.sem_inc(once["swa_operands"], 1)
            dve.wait_ge(once["silu2"], 1)
            attend(SWA, lambda h, qt: rq[:, 32 * qt + h:32 * qt + h + 1])
            residual_blocks("g_mix")

            for b in range(2):
                splits(8)
                if b == 0:
                    token_norm(2)
                times_rs(lambda k: V3T[:, 4 * b + k:4 * b + k + 2, :])
            with loop(dve, 7, rounds) as i:
                for b in range(2):
                    splits(8)
                    times_rs(lambda k: S[:, bass.ds(8 * i + (4 * b + k), 2), :])
            for k in range(4):
                dve.wait_ge(once[f"v3_transposed{k}"], 1)
                dve.tensor_copy(V3[:, k % 2, 4 * (k // 2):4 * (k // 2) + 4, :], PT[:, :, :])\
                   .then_inc(once[f"v3_taken{k}"], 1)
            dve.wait_ge(psum_free, blk.value)
            attend(MOBA, lambda h, qt: MHD ** -0.5, gate=False)

            def taps(dst, src, name, n, bias=None):
                for t in range(HALF):
                    w = col(name, HALF * (n - 1) + t)
                    if bias is None:
                        ins = dve.tensor_scalar(dst[:, t, :], src[:, t, :], w, None, ALU.mult)
                    else:
                        ins = dve.tensor_scalar(dst[:, t, :], src[:, t, :], w, col(bias, t), ALU.mult, ALU.add)
                step(ins)
                for d in range(1, n):
                    for t in range(HALF):
                        ins = dve.scalar_tensor_tensor(out=dst[:, t, d:], in0=src[:, t, 0:T - d],
                                                       scalar=col(name, HALF * (n - 1 - d) + t),
                                                       in1=dst[:, t, d:], op0=ALU.mult, op1=ALU.add)
                    step(ins)

            step(dve.tensor_tensor(S[:, 40:48, :], S[:, 40:48, :], S[:, 48:56, :], ALU.mult))
            taps(S[:, 48:56, :], S[:, 40:48, :], "sc_w", 3)
            dve.tensor_tensor(S[:, 48:56, :], S[:, 48:56, :], S[:, 32:40, :], ALU.mult).then_inc(once["sc_ready"], 1)
            taps(S[:, 0:8, :], S[:, 16:24, :], "conv_w", 4, "conv_b")
            dve.sem_inc(once["xc_ready"], 1)
            dve.wait_ge(once["sc_hi"], 1)
            dve.tensor_tensor(SCL[:, :, :], S[:, 48:56, :], SCH[:, :, :].bitcast(F32), ALU.subtract)\
               .then_inc(once["sc_lo"], 1)
            dve.wait_ge(once["xc_hi"], 1)
            dve.tensor_tensor(XCL[:, :, :], S[:, 0:8, :], XCH[:, :, :].bitcast(F32), ALU.subtract)\
               .then_inc(once["xc_lo"], 1)
            lam = col("lam", 0, HALF)
            dve.scalar_tensor_tensor(out=SP8[:, 0, :], in0=lam, scalar=-1.0, in1=lam, op0=ALU.mult, op1=ALU.max)\
               .then_inc(once["abs_lam"], 1)
            dve.wait_ge(once["exp_lam"], 1)
            e, y, y2, acc = SP8[:, 1, :], SP8[:, 2, :], SP8[:, 3, :], SP8[:, 4, :]
            step(dve.tensor_scalar(y, e, 2.0, None, ALU.add))
            step(dve.reciprocal(y2, y))
            step(dve.tensor_tensor(y, e, y2, ALU.mult))
            step(dve.tensor_tensor(y2, y, y, ALU.mult))
            step(dve.tensor_scalar(acc, y2, 1.0 / (2 * LN1P_TERMS + 1), None, ALU.mult))
            for k in range(LN1P_TERMS - 1, 0, -1):
                step(dve.scalar_tensor_tensor(out=acc, in0=acc, scalar=1.0 / (2 * k + 1), in1=y2, op0=ALU.add,
                                              op1=ALU.mult))
            step(dve.scalar_tensor_tensor(out=acc, in0=acc, scalar=1.0, in1=y, op0=ALU.add, op1=ALU.mult))
            step(dve.tensor_scalar(y, lam, -1.0, 0.0, ALU.mult, ALU.max))
            step(dve.scalar_tensor_tensor(out=acc, in0=acc, scalar=2.0, in1=y, op0=ALU.mult, op1=ALU.add))
            dve.tensor_scalar(SP8[:, 6, :], acc, -8.0, None, ALU.mult)
            dve.tensor_scalar(SP8[:, 7, :], acc, 8.0, None, ALU.mult).then_inc(once["sp_ready"], 1)
            splits(2)
            blk.add(4)
            used.add(2)
            dve.wait_ge(once["a_squared"], 1)
            dve.scalar_tensor_tensor(out=LRU_M[:, :, :], in0=S[:, 8:16, :], scalar=1.0, in1=LRU_M[:, :, :],
                                     op0=ALU.add, op1=ALU.mult).then_inc(once["m2_ready"], 1)
            dve.wait_ge(once["mult_ready"], 1)
            step(dve.scalar_tensor_tensor(out=S[:, 16:24, :], in0=LRU_M[:, :, :], scalar=2.0 ** -50,
                                          in1=S[:, 16:24, :], op0=ALU.mult, op1=ALU.mult))
            step(dve.tensor_tensor(S[:, 0:8, :], S[:, 0:8, :], S[:, 16:24, :], ALU.mult))
            for t in range(HALF):
                ins = dve.tensor_tensor_scan(out=S[:, 8 + t, :], data0=LRU_A[:, t, :], data1=S[:, t, :],
                                             initial=0.0, op0=ALU.mult, op1=ALU.add)
            step(ins)
            dve.wait_ge(once["gelu_ready"], 1)
            dve.tensor_tensor(S[:, 24:32, :], S[:, 24:32, :], S[:, 8:16, :], ALU.mult).then_inc(once["lru_ready"], 1)
            g_lo(GL[:, 8:16, :], S[:, 24:32, :], GH[:, 8:16, :])
            for branch in range(3):
                last = branch == 2
                steps = [(sub, 24), (used, 24), (blk, 4), (gr, 2)]
                steps += [(gh, 2)] * last
                with loop(dve, 2, steps) as i:
                    for b in range(2):
                        t0 = 8 * i + 4 * b
                        splits(8)
                        times_rs(lambda k: MT[:, k:k + 2, :])
                        splits(4)
                        ps = block_done(4)
                        dve.wait_ge(gate_ready, gr.add())
                        for k in (0, 2):
                            dst = MT[:, k:k + 2, :] if branch else MIX[:, bass.ds(t0 + k, 2), :]
                            ins = dve.tensor_tensor(dst, ps[:, k:k + 2], SG[:, k:k + 2, :], ALU.mult)
                        ins.then_inc(psum_free, 1)
                        if branch:
                            mix = MIX[:, bass.ds(t0, 4), :]
                            dve.wait_ge(psum_free, blk.value)
                            ins = dve.tensor_tensor(mix, mix, MT[:, :, :], ALU.add)
                            if last:
                                ins.then_inc(mix_ready, 1)
                                g_lo(GL[:, bass.ds(t0, 4), :], mix, GH[:, bass.ds(t0, 4), :])
            residual_blocks("g_mlp")

            def hidden(t0):
                times_rs(lambda k: UT[:, k:k + 2, :])
                dve.wait_ge(psum_free, blk.value)
                dve.scalar_tensor_tensor(out=UU, in0=UT, scalar=0.0, in1=UT, op0=ALU.max, op1=ALU.mult)\
                   .then_inc(hidden_ready, 1)
                g_lo(GL[:, bass.ds(t0, 4), :], UU, GH[:, bass.ds(t0, 4), :])

            for g in range(4):
                if g == 0:
                    splits(8)
                    token_norm(3)
                    hidden(0)
                    for b in range(1, 4):
                        splits(8)
                        hidden(4 * b)
                else:
                    with loop(dve, 2, rounds + [(gh, 2)]) as i:
                        for b in range(2):
                            splits(8)
                            hidden(8 * i + 4 * b)
                if g < 3:
                    with loop(dve, 2, rounds) as i:
                        for b in range(2):
                            splits(8)
                            add_residual(8 * i + 4 * b)
            for b in range(4):
                splits(min(8, n_subs - sub.base))
                add_residual(4 * b)
            token_norm(4)
            for t in range(NT):
                ins = dve.scalar_tensor_tensor(out=S[:, 16 + t, :], in0=X[:, t, :], scalar=col("g_final", t),
                                               in1=rs[:, :], op0=ALU.mult, op1=ALU.mult)
                if t % 4 == 3:
                    ins.then_inc(out_ready, 1)

        @block.gpsimd
        def _(pool):
            steps_n = Count(pool_step)

            def step(ins):
                ins.then_inc(pool_step, 1)
                pool.wait_ge(pool_step, steps_n.add())

            def squares(n, ready):
                if n:
                    pool.wait_ge(ssq_done, n)
                for j in range(4):
                    pool.wait_ge(*ready(j))
                    for k in range(4 * j, 4 * j + 4, 2):
                        x = X[:, k:k + 2, :]
                        if k == 0:
                            step(pool.tensor_tensor(SQACC[:, :, :], x, x, ALU.mult))
                        else:
                            step(pool.tensor_tensor(SQTMP[:, :, :], x, x, ALU.mult))
                            step(pool.tensor_tensor(SQACC[:, :, :], SQACC[:, :, :], SQTMP[:, :, :], ALU.add))
                pool.sem_inc(sq_ready, 1)

            def load_biases(a, chunks):
                for chunk in chunks:
                    gc = a.row0 // 4 + chunk
                    if chunk >= 2:
                        u = a.units.index((chunk - 2, 0, (chunk - 2) % a.per == a.per - 1))
                        pool.wait_ge(log_free, BEFORE[a][1] + a.n_banks(u + 1))
                    src = bass.AP(bias_rows, (a.row0 + 4 * chunk) * bias_head + P - 1,
                                  [[ROWS, P], [bias_head, 4], [1, T]])
                    pool.dma_start(BBUF[a][:, gc % 2], src).then_inc(bias_in[gc % 2], 16)

            step(pool.memset(ones[:, :], 1.0))
            step(pool.memset(pair[:, :], 0.0))
            for a in range(2):
                step(pool.memset(pair[HD * a:HD * a + HD, a:a + 1], 1.0))
            pool.sem_inc(consts_set, 1)
            squares(0, lambda j: (x_in_sem[j], 16))
            pool.wait_ge(rows_copied, 1)
            row = 0
            for k, n in enumerate((DSA_HEADS, SWA_HEADS, MOBA_HEADS)):
                pool.dma_start(bias_rows.ap()[row:row + n, :, 0:ROWS],
                               ROWS_SB[0:n, k, None, :].to_broadcast([n, P, ROWS])).then_inc(rows_stored, 16)
                row += n
            pool.wait_ge(rows_stored, 48)
            load_biases(DSA, (0, 1))
            pool.wait_ge(score_ready, 1)
            s = SCORE[:, P:].rearrange("p (a k) -> p a k", a=2)
            pool.affine_select(out=s, in_=s, compare_op=ALU.is_ge, fill=FUTURE, base=0,
                               pattern=[[0, 2], [-1, P]], channel_multiplier=1).then_inc(score_causal, 1)
            load_biases(DSA, (2, 3))
            pool.wait_ge(subs_used, POOL_SUBS)
            load_biases(SWA, (0, 1))
            squares(1, lambda j: (psum_free, L1_BLOCKS - 3 + j))
            load_biases(SWA, range(2, 8))
            squares(2, lambda j: (psum_free, L2_BLOCKS - 3 + j))
            load_biases(MOBA, (0, 1))
            squares(3, lambda j: (psum_free, MIX_BLOCK + 24 + 1 + j))
            squares(4, lambda j: (psum_free, MIX_BLOCK + 24 + 4 + 28 + 1 + j))


def buckets(max_distance):
    n = np.arange(T)
    large = 16 + (np.log(np.maximum(n, 1).astype(np.float32) / np.float32(16))
                  / np.float32(math.log(max_distance / 16)) * np.float32(16)).astype(np.int32)
    return np.where(n < 16, n, np.minimum(large, 31))


def shape_constants():
    onehot = np.zeros((33, 3, ROWS), np.float32)
    for k, (far, window) in enumerate(((1024, T), (1024, P), (128, T))):
        b = buckets(far)
        for m in range(ROWS):
            n = T - 1 - m
            if 0 <= n < window:
                onehot[b[n], k, m] = 1.0
            else:
                onehot[32, k, m] = NEG
    const = np.zeros((P, P + 64), np.float32)
    const[:, 0:P] = np.eye(P)
    for g, w in enumerate(POOL_WINDOWS):
        const[:, P + 16 * g:P + 16 * g + 16] = 1.0 / np.minimum(np.arange(16) + 1, w)
    return onehot, const


def blocks(w, cols):
    w = w[:, cols]
    k, n = w.shape
    w = w.reshape(k // (2 * P), 2, P, n // BLK, BLK).transpose(3, 0, 2, 1, 4)
    return w.reshape(-1, P, SUB)


def weight_stream(a):
    f = {n: np.asarray(v, np.float32)[0] for n, v in a.items() if np.ndim(v) > 2}
    r = lambda at, n: slice(at, at + n)
    w = f["even_w_in"]
    keys = np.concatenate([w[:, 3072:3200], w[:, 5248:5328], np.zeros((D, 48), np.float32)], axis=1)
    subs = [keys.reshape(4, 4, P, 256).transpose(0, 2, 1, 3).reshape(4, P, SUB)]
    subs += [blocks(w, r(at, 1024)) for at in (4224, 2048, 3200, 0, 1024)]
    pw = f["even_pool_w"].reshape(2, 2, 2, P, 256)
    subs += [pw.transpose(0, 3, 1, 2, 4).reshape(2, P, SUB), blocks(f["even_w_out"], r(0, D))]
    w = f["odd_w_in"]
    subs += [blocks(w, r(2048, 512)), blocks(w, r(0, 2048)), blocks(w, r(2560, 2048)),
             blocks(f["odd_w_out"], r(0, D))]
    w = f["w_in_2"]
    subs += [blocks(w, r(2048, 1024)), blocks(w, r(0, 2048)), blocks(w, r(3072, 5 * 1024))]
    ga, gx = (f[n].reshape(2, 4, P, P).transpose(0, 2, 1, 3).reshape(2, P, 512) for n in ("lru_wa_2", "lru_wx_2"))
    subs += [np.concatenate([ga, gx], axis=2)]
    for k, n in enumerate(("w_attn_o_2", "w_lru_o_2", "w_sc_o_2")):
        gates = blocks(w, r(8192 + D * k, D)).reshape(4, 8, P, SUB)
        outs = blocks(f[n], r(0, D)).reshape(4, 4, P, SUB)
        subs += [np.concatenate([gates, outs], axis=1).reshape(-1, P, SUB)]
    subs += [blocks(f["w_out_2"], r(0, D))]
    up = blocks(f["w_mlp_up_2"], r(0, 4 * D)).reshape(4, 32, P, SUB)
    for g in range(4):
        subs += [up[g], blocks(f["w_mlp_down_2"][D * g:D * g + D], r(0, D))]
    return np.concatenate(subs, axis=0)


def tiles(v):
    return np.asarray(v, np.float32).reshape(-1, P).T


def kernel(**a):
    import concourse.bacc as bacc
    from concourse.bass_utils import run_bass_kernel_spmd

    onehot, const = shape_constants()
    twice = lambda v: np.tile(np.asarray(v, np.float32).reshape(HD, 1), (2, 1))
    small = np.concatenate(
        [tiles(a[n][0]) for n in ("even_norm", "odd_norm", "norm_mix_g_2", "norm_mlp_g_2")]
        + [tiles(a["final_g_2"]), tiles(a["even_pool_scale"][0])]
        + [twice(a[n][0]) for n in ("even_q_gain", "even_k_gain", "odd_q_gain", "odd_k_gain")]
        + [tiles(a["gate_b_2"][0])] + [tiles(v) for v in a["lru_conv_w_2"][0]]
        + [tiles(a[n][0]) for n in ("lru_conv_b_2", "lru_ba_2", "lru_bx_2", "lru_lambda_2")]
        + [tiles(v) for v in a["sc_conv_w_2"][0]]
        + [np.broadcast_to(np.asarray(a["odd_sinks"][0], np.float32), (P, SWA_HEADS))], axis=1)
    rel, rel2 = np.asarray(a["rel_bias"], np.float32), np.asarray(a["rel_table_2"], np.float32)
    tables = np.zeros((33, 96), np.float32)
    tables[0:32, 0:16], tables[0:32, 32:64], tables[0:32, 64:72] = rel[:, 0:16], rel, rel2
    tables[32] = 1.0
    x = np.asarray(a["x"], np.float32)[0].T.reshape(NT, P, T).transpose(1, 0, 2)
    arrays = {"x": x, "w": weight_stream(a), "small": small, "tables": tables, "onehot": onehot,
              "const": const}
    arrays = {n + "_dram": np.ascontiguousarray(v, dtype=np.float32) for n, v in arrays.items()}
    nc = bacc.Bacc("TRN2", target_bir_lowering=False, num_devices=1)
    ins = [nc.dram_tensor(n, v.shape, F32, kind="ExternalInput").ap() for n, v in arrays.items()]
    out = nc.dram_tensor("y_dram", [P, NT, T], F32, kind="ExternalOutput").ap()
    build(nc, *ins, out)
    r = run_bass_kernel_spmd(nc, [arrays], core_ids=[0])
    y = r.results[0]["y_dram"]
    return np.ascontiguousarray(y.transpose(2, 1, 0)).reshape(1, T, D)
```

```python
import math
from contextlib import ExitStack, contextmanager

import numpy as np

import concourse.bass as bass
from concourse import mybir

F32 = mybir.dt.float32
F32R = mybir.dt.float32r
ALU = mybir.AluOpType
ACT = mybir.ActivationFunctionType
AX_X = mybir.AxisListType.X

P = 128
T = 256
D = 2048
NT = D // P
HALF = NT // 2
UNIT = HALF * T
EPS = 1e-6
NEG = -1.0e30
SUB = 1024
AHEAD = 4
BLK = 4 * P

DSA_HEADS, SWA_HEADS, MOBA_HEADS = 16, 32, 8
HD = 64
MHD = 128
TOPK = 64
TAKEN = -3.0e38
FUTURE = -1.0e38
ROWS = 384
LN1P_TERMS = 11
POOL_WINDOWS = (2, 4, 8, 16)

L1_PROJ = 1 + 10
L1_BLOCKS = L1_PROJ + 2 + 4
L2_BLOCKS = L1_BLOCKS + 9 + 4
L3_BLOCKS = L2_BLOCKS + 16
MIX_BLOCK = L3_BLOCKS

L1_INDEX, L1_QUERIES, L1_ATTEND, L1_POOL = 16, 32, 48, 80
L2_ORDER = ("q0", "q1", "g0", "q2", "g1", "q3", "g2", "g3")
L2_SUMS = (10, 24, 40, 53)
L2_START = (13, 27, 43, 56)
L3_CONV, L3_GATES, L3_LRU, L3_SC = 28, 48, 59, 48
L1_OUT_TILES = (8, 9, 10, 11, 0, 1, 2, 3, 4, 5, 6, 7, 12, 13, 14, 15)

SMALL = {}
N_SMALL = 0
for _name, _n in (("g_even", NT), ("g_odd", NT), ("g_mix", NT), ("g_mlp", NT), ("g_final", NT),
                  ("pool_scale", HALF), ("dsa_q", 1), ("dsa_k", 1), ("swa_q", 1), ("swa_k", 1),
                  ("gate_b", 3 * NT), ("conv_w", 4 * HALF), ("conv_b", HALF), ("ba", HALF),
                  ("bx", HALF), ("lam", HALF), ("sc_w", 3 * HALF), ("sinks", SWA_HEADS)):
    SMALL[_name] = N_SMALL
    N_SMALL += _n


class Count:

    def __init__(self, sem):
        self.sem, self.base, self.i, self.step = sem, 0, None, 0

    @property
    def value(self):
        return self.base if self.i is None else self.i * self.step + self.base

    def add(self, n=1):
        self.base += n
        return self.value


@contextmanager
def loop(eng, n, steps):
    starts = [c.base for c, _ in steps]
    with eng.Fori(0, n) as i:
        for c, step in steps:
            c.i, c.step = i, step
        yield i
    for (c, step), start in zip(steps, starts):
        assert c.base == start + step, (c.sem, c.base - start, step)
        c.base, c.i = start + n * step, None


class Attention:

    def __init__(self, heads, hd, row0, at):
        self.heads, self.hd, self.row0, self.at = heads, hd, row0, at
        self.per = 512 // (4 * hd)
        self.units = [(g * self.per + c, qt, c == self.per - 1)
                      for g in range(heads // 4 // self.per) for qt in (1, 0) for c in range(self.per)]

    def banks(self, u):
        return [[0, 2], [1, 3]]

    def packs(self, u):
        blocks = [(h, kt) for h in range(4) for kt in range(self.units[u][1] + 1)]
        return [blocks[k:k + 4] for k in range(0, len(blocks), 4)]

    def n_banks(self, u):
        return sum(len(self.banks(v)) for v in range(u))

    def n_packs(self, u):
        return sum(len(self.packs(v)) for v in range(u))

    def n_flushes(self, u):
        return sum(last for *_, last in self.units[:u])

    def due(self, tick):
        return [(u, tick - at, (tick - at - 7 - self.units[u][1]) if self.units[u][2] else None)
                for u, at in enumerate(self.at) if 0 <= tick - at <= 12]


def index_banks(qt):
    n = 4 // (qt + 1)
    return [[h0 + 2 * m + odd for m in range(n)] for h0 in range(0, DSA_HEADS, 2 * n) for odd in range(2)]


DSA = Attention(DSA_HEADS, HD, 0, [L1_ATTEND + 2 + n for n in (0, 4, 7, 11, 13, 17, 20, 24)])
SWA = Attention(SWA_HEADS, HD, DSA_HEADS,
                [start + n for start in L2_START for n in ((0, 4, 8, 11) if start < L2_START[3] else (0, 3, 6, 8))])
MOBA = Attention(MOBA_HEADS, MHD, DSA_HEADS + SWA_HEADS, [5, 12, 19, 26])
BEFORE = {}
_u = _b = _p = _f = 0
for _a in (DSA, SWA, MOBA):
    BEFORE[_a] = (_u, _b, _p, _f)
    _n = len(_a.units)
    _u, _b, _p, _f = _u + _n, _b + _a.n_banks(_n), _p + _a.n_packs(_n), _f + _a.n_flushes(_n)


def build(nc, x_in, w_in, small_in_dram, tables_in, onehot_in, const_in, out):
    n_subs = w_in.shape[0]
    bias_rows = nc.dram_tensor("bias_rows", [DSA_HEADS + SWA_HEADS + MOBA_HEADS, P, ROWS + 1], F32,
                               kind="Internal")
    bias_head = P * (ROWS + 1)
    place = [-(-nc.sbuf_base // 64) * 64]

    def fixed(name, shape, dt=F32):
        t = nc.alloc_sbuf_tensor_at(name, shape, dt, offset=place[0])
        place[0] += -(-4 * int(np.prod(shape[1:])) // 32) * 32
        assert place[0] <= nc.sbuf_usable_end, (name, place[0])
        return t

    def view(name, shape, offset, dt=F32):
        return nc.alloc_sbuf_tensor_at(name, shape, dt, offset=offset)

    with ExitStack() as ctx:
        def sem(name):
            return ctx.enter_context(nc.semaphore(name))

        X = fixed("X", [P, NT, T])
        RAW = fixed("RAW", [P, AHEAD, SUB])
        WH = fixed("WH", [P, AHEAD, SUB], F32R)
        WL = fixed("WL", [P, AHEAD, SUB], F32R)
        HH = fixed("HH", [P, NT, T], F32R)
        HL = fixed("HL", [P, NT, T], F32R)
        g_at = place[0]
        GH = fixed("GH", [P, NT, T], F32R)
        GL = fixed("GL", [P, NT, T], F32R)
        s_at = place[0]
        S = fixed("S", [P, 8 * HALF, T])
        small = fixed("small", [P, N_SMALL])
        ident = fixed("ident", [P, P])
        ones = fixed("ones", [P, P])
        pair = fixed("pair", [P, 2])
        rs = fixed("rs", [P, T])
        SQACC = fixed("SQACC", [P, 2, T])
        SQTMP = fixed("SQTMP", [P, 2, T])
        pts_at = place[0]
        pts = fixed("pts", [P, 2, 512])
        TF = fixed("TF", [P, 512])
        o_sb = fixed("o_sb", [P, 512])
        rq_at = place[0]
        rq = fixed("rq", [P, 64])
        neg_max = fixed("neg_max", [P, 4, 4])
        sums = fixed("sums", [P, 2, 8])
        r_sums = fixed("r_sums", [P, 8])
        sink_d = fixed("sink_d", [P, 4, 4])
        sink_e = fixed("sink_e", [P, 2, 8])
        q_var = fixed("q_var", [P, 2, 16])
        gg = fixed("gg", [P, 2])

        def unit(k):
            return s_at + 4 * UNIT * k

        def gunit(k):
            return g_at + 4 * UNIT * k

        def col(name, k=0, n=1):
            a = SMALL[name] + k
            return small[:, a:a + n]

        TABS = view("TABS", [33, 96], unit(7) + 4 * 3 * ROWS)
        ONEHOT = view("ONEHOT", [33, 3, ROWS], unit(6))
        ROWS_SB = view("ROWS_SB", [32, 3, ROWS], unit(7))
        EA, EB, KT1, IKT = S[:, 40, :], S[:, 41, :], S[:, 42, :], S[:, 43, :]
        V1 = view("V1", [P, 2, P], unit(5) + 16 * T)
        IW = view("IW", [P, 2, P], unit(5) + 20 * T)
        SCORE = view("SCORE", [P, 384], unit(5) + 24 * T)
        TOP8 = view("TOP8", [P, 2, 8], unit(5) + 30 * T)
        INV = view("INV", [P, 4, 16], unit(5) + 30 * T + 64)
        RELU = view("RELU", [P, 2, 512], gunit(0))
        SQ1 = view("SQ1", [P, HALF, T], gunit(2))
        KSQ1 = view("KSQ1", [P, T], gunit(0) + 16 * T)
        RK1 = view("RK1", [P, T], gunit(0) + 20 * T)
        WINDOW = [view(f"WINDOW{k}", [P, HALF, T], gunit(2 * k)) for k in range(2)]
        K2 = view("K2", [P, 4, T], unit(4))
        V2 = view("V2", [P, 2, 2, P], unit(4) + 16 * T)
        KV2 = view("KV2", [P, 4, T], unit(5))
        KSQ2 = view("KSQ2", [P, 2, T], unit(5) + 16 * T)
        RK2 = view("RK2", [P, 2, T], unit(5) + 24 * T)
        SQ2 = view("SQ2", [P, 4, T], unit(7))
        V3T = view("V3T", [P, HALF, T], gunit(0))
        V3 = view("V3", [P, 2, HALF, P], gunit(3))
        SCH = view("SCH", [P, HALF, T], unit(5), F32R)
        SCL = view("SCL", [P, HALF, T], unit(6), F32R)
        XCH = view("XCH", [P, HALF, T], gunit(1), F32R)
        XCL = view("XCL", [P, HALF, T], gunit(3), F32R)
        LRU_I = view("LRU_I", [P, HALF, T], gunit(1))
        LRU_A = view("LRU_A", [P, HALF, T], gunit(3))
        LRU_A2 = view("LRU_A2", [P, HALF, T], pts_at)
        LRU_M = S[:, 24:32, :]
        XC = S[:, 56:64, :]
        SP8 = view("SP8", [P, 8, HALF], rq_at)
        MIX = S[:, 0:16, :]
        SG = S[:, 16:20, :]
        MT = S[:, 20:24, :]
        UT = S[:, 0:4, :]
        UU = S[:, 4:8, :]
        LAST_SQ = S[:, 8:12, :]
        LBUF = {a: view(f"L{n}", [P, 2, 4, T], o) for n, (a, o) in
                enumerate(((DSA, unit(7)), (SWA, unit(5)), (MOBA, gunit(1))))}
        BBUF = {a: view(f"B{n}", [P, 2, 4, T], o) for n, (a, o) in
                enumerate(((DSA, unit(6)), (SWA, unit(6)), (MOBA, unit(7))))}

        GP = ctx.enter_context(nc.psum_tensor("GP", [P, 2, 4, T], F32))
        LOG = ctx.enter_context(nc.psum_tensor("LOG", [P, 2, 512], F32))
        PT = ctx.enter_context(nc.psum_tensor("PT", [P, 4, P], F32))
        OP = ctx.enter_context(nc.psum_tensor("OP", [P, 512], F32))

        def gate_sums(gate, n):
            if gate == 0:
                return LOG[:, n // 2, (n % 2) * T:(n % 2 + 1) * T]
            return OP[:, (n % 2) * T:(n % 2 + 1) * T] if n >= 2 else PT[:, 2 * n:2 * n + 2, :].rearrange("p b q -> p (b q)")

        raw_full = [sem(f"raw_full{k}") for k in range(AHEAD)]
        hi_ready, lo_ready, subs_used = sem("hi_ready"), sem("lo_ready"), sem("subs_used")
        psum_free = sem("psum_free")
        consts_in = sem("consts_in")
        small_in, sq0_ready = sem("small_in"), sem("sq0_ready")
        x_in_sem = [sem(f"x_in{k}") for k in range(4)]
        hh_ready, hl_ready = sem("hh_ready"), sem("hl_ready")
        gh_ready, gl_ready = sem("gh_ready"), sem("gl_ready")
        sq_ready, ssq_done = sem("sq_ready"), sem("ssq_done")
        var_ready, std_ready = sem("var_ready"), sem("std_ready")
        gate_ready = sem("gate_ready")
        dve_step, pool_step, act_step = sem("dve_step"), sem("pool_step"), sem("act_step")
        consts_set = sem("consts_set")
        rows_done, rows_copied, rows_stored = sem("rows_done"), sem("rows_copied"), sem("rows_stored")
        bias_in = [sem("bias_in0"), sem("bias_in1")]
        idx_ready, idx_free, relu_used = sem("idx_ready"), sem("idx_free"), sem("relu_used")
        score_ready, score_causal = sem("score_ready"), sem("score_causal")
        log_ready, log_free = sem("log_ready"), sem("log_free")
        max_ready, p_ready = sem("max_ready"), sem("p_ready")
        pt_ready, pt_taken, pv_done = sem("pt_ready"), sem("pt_taken"), sem("pv_done")
        o_ready, ot_ready, ot_taken = sem("o_ready"), sem("ot_ready"), sem("ot_taken")
        out_ready, out_done = sem("out_ready"), sem("out_done")
        mix_ready, hidden_ready = sem("mix_ready"), sem("hidden_ready")
        q2_squared, q2_summed, q2_taken = sem("q2_squared"), sem("q2_summed"), sem("q2_taken")
        silu2, kv_head_ready = sem("silu2"), sem("kv_head_ready")
        once = {n: sem(n) for n in (
            "va_transposed", "va_taken", "ksq1", "ksq1_summed", "q1_squared", "q1_summed",
            "dsa_operands", "silu1", "silu_pool", "pooled", "pooled_hi", "pooled_lo",
            "v2_transposed", "v2_taken", "ksq2", "ksq2_summed",
            "v3_transposed0", "v3_transposed1", "v3_transposed2", "v3_transposed3",
            "v3_taken0", "v3_taken1", "v3_taken2", "v3_taken3",
            "sc_ready0", "sc_hi0", "sc_lo0", "sc_ready1", "sc_hi1", "sc_lo1", "xc_ready", "xc_hi", "xc_lo", "abs_lam", "exp_lam",
            "sp_ready", "lru_taken", "decays", "a_squared", "m2_ready", "mult_ready", "gelu_ready",
            "lru_ready", "last_squares")}

        block = ctx.enter_context(nc.Block())

        @block.sync
        def _(sp):
            for k in range(AHEAD):
                sp.dma_start(RAW[:, k, :], w_in[k]).then_inc(raw_full[k], 16)
            with sp.Fori(1, n_subs // AHEAD) as i:
                for k in range(AHEAD):
                    sp.wait_ge(lo_ready, AHEAD * i + (k + 1 - AHEAD))
                    sp.dma_start(RAW[:, k, :], w_in[AHEAD * i + k]).then_inc(raw_full[k], 16)
            for n in range(4):
                sp.wait_ge(out_ready, n + 1)
                sp.dma_start(out[:, 4 * n:4 * n + 4, :], S[:, 16 + 4 * n:20 + 4 * n, :]).then_inc(out_done, 16)
            sp.wait_ge(out_done, 64)

        @block.tensor
        def _(pe):
            sub, blk = Count(subs_used), Count(psum_free)
            pt_free = [None]

            def three(o, wh, wl, rh, rl, start, stop):
                pe.matmul(o, wh, rh, start=start, stop=False, skip_group_check=True)
                pe.matmul(o, wh, rl, start=False, stop=False, skip_group_check=True)
                return pe.matmul(o, wl, rh, start=False, stop=stop, skip_group_check=True)

            def take_sub():
                pe.wait_ge(lo_ready, sub.value + 1)
                return sub.base % AHEAD

            def open_block():
                if blk.base >= 2:
                    pe.wait_ge(psum_free, blk.value - 1)
                blk.add()
                return GP[:, (blk.base - 1) % 2]

            def gemm(RH, RL, nkt=NT, k0=0, kts=2, n_out=4, ready=None, tick=None):
                ps = open_block()
                for j in range(nkt // kts):
                    if ready is not None and (j * kts) % 4 == 0:
                        pe.wait_ge(ready[0], ready[1] + (j * kts) // 4 + 1)
                    slot = take_sub()
                    wh = WH[:, slot].rearrange("p (k n) -> p k n", k=kts)
                    wl = WL[:, slot].rearrange("p (k n) -> p k n", k=kts)
                    for k in range(kts):
                        kt = j * kts + k
                        for n in range(n_out):
                            c = slice(n * P, (n + 1) * P)
                            mm = three(ps[:, n], wh[:, k, c], wl[:, k, c], RH[:, k0 + kt], RL[:, k0 + kt],
                                       start=(kt == 0 and n % 2 == 0), stop=(kt == nkt - 1))
                    mm.then_inc(subs_used, 1)
                    sub.add()
                    if tick:
                        tick(j)

            def gemm_pair(RH, RL, tiles, waits, tick):
                halves, n = [], 0
                for b, pairs in ((0, range(6)), (1, range(6)), (0, (6, 7)), (1, (6, 7))):
                    if pairs[0] == 0:
                        halves.append(open_block())
                    for j in pairs:
                        if b == 0 and j % 2 == 0:
                            pe.wait_ge(gl_ready, waits[j // 2])
                        slot = take_sub()
                        wh = WH[:, slot].rearrange("p (k n) -> p k n", k=2)
                        wl = WL[:, slot].rearrange("p (k n) -> p k n", k=2)
                        for k in range(2):
                            kt = tiles[2 * j + k]
                            for m in range(4):
                                c = slice(m * P, (m + 1) * P)
                                mm = three(halves[b][:, m], wh[:, k, c], wl[:, k, c], RH[:, kt], RL[:, kt],
                                           start=(j == 0 and k == 0 and m % 2 == 0), stop=(j == 7 and k == 1))
                        mm.then_inc(subs_used, 1)
                        sub.add()
                        tick(n)
                        n += 1

            def gemms(n, RH, RL):
                with loop(pe, n, [(sub, 4 * AHEAD), (blk, 2)]):
                    for _ in range(2):
                        gemm(RH, RL)

            def ssq(n):
                pe.wait_ge(sq_ready, n + 1)
                pe.matmul(OP[:, 0:T], ones[:, :], SQACC[:, 0, :], start=True, stop=False)
                pe.matmul(OP[:, 0:T], ones[:, :], SQACC[:, 1, :], start=False, stop=True)\
                  .then_inc(ssq_done, 1)

            def transposes(src, wait, done, free):
                pe.wait_ge(*wait)
                if pt_free[0]:
                    pe.wait_ge(*pt_free[0])
                for b, ap in enumerate(src):
                    mm = pe.transpose(PT[:, b, :], ap, ident[:, :])
                mm.then_inc(done, 1)
                pt_free[0] = free

            def attend(a, tick, q_of, k_of, v_of):
                u0, bank0, pk0, f0 = BEFORE[a]
                L = LBUF[a]
                for u, d, flush in reversed(a.due(tick)):
                    chunk, qt, _ = a.units[u]
                    nk, packs = P * (qt + 1), a.packs(u)
                    bank, pk, fl = bank0 + a.n_banks(u), pk0 + a.n_packs(u), f0 + a.n_flushes(u)
                    if d == 0:
                        for heads in a.banks(u):
                            if bank >= 2:
                                pe.wait_ge(log_free, bank - 1)
                            for m, h in enumerate(heads):
                                mm = pe.matmul(LOG[:, bank % 2, m * nk:(m + 1) * nk],
                                               q_of(4 * chunk + h, qt), k_of(4 * chunk + h, nk),
                                               start=True, stop=True, skip_group_check=True)
                            mm.then_inc(log_ready, 1)
                            bank += 1
                    if d - 5 in range(len(packs)):
                        k = d - 5
                        transposes([L[:, u % 2, h, kt * P:(kt + 1) * P] for h, kt in packs[k]],
                                   (p_ready, u0 + u + 1), pt_ready, (pt_taken, pk + k + 1))
                    if d - 6 in range(len(packs)):
                        k = d - 6
                        pe.wait_ge(pt_taken, pk + k + 1)
                        if k == 0 and chunk % a.per == 0 and fl:
                            pe.wait_ge(o_ready, fl)
                        for b, (h, kt) in enumerate(packs[k]):
                            c = (4 * (chunk % a.per) + h) * a.hd
                            mm = pe.matmul(OP[:, c:c + a.hd], pts[:, (pk + k) % 2, b * P:(b + 1) * P],
                                           v_of(4 * chunk + h, kt), start=(c == 0 and kt == 0),
                                           stop=(kt == qt), skip_group_check=True)
                        mm.then_inc(pv_done, 1)
                    if flush == 2:
                        transposes([o_sb[:, b * P:(b + 1) * P] for b in range(4)],
                                   (o_ready, fl + 1), ot_ready, (ot_taken, fl + 1))

            def bias_tables():
                pe.wait_ge(consts_in, 16 * 4)
                pe.wait_ge(psum_free, 1)
                for k, o in enumerate((LOG[0:32, 0, 0:ROWS], LOG[0:32, 1, 0:ROWS], OP[0:32, 0:ROWS])):
                    mm = pe.matmul(o, TABS[0:33, 32 * k:32 * k + 32], ONEHOT[0:33, k, :], start=True, stop=True)
                mm.then_inc(rows_done, 1)

            gemm(HH, HL, kts=4, n_out=2, ready=(hl_ready, 0))
            pe.wait_ge(consts_set, 1)
            ssq(0)

            def half_rows(tile_of):
                return lambda h, qt: S[HD * (h % 2):HD * (h % 2) + HD, tile_of(h), qt * P:(qt + 1) * P]

            def index(n):
                if n == 0:
                    pe.wait_ge(psum_free, 3)
                if n >= 2:
                    pe.wait_ge(idx_free, n - 1)
                qt, heads = [(qt, heads) for qt in (1, 0) for heads in index_banks(qt)][n]
                nk = P * (qt + 1)
                for m, h in enumerate(heads):
                    r = slice(HD * (h % 2), HD * (h % 2) + HD)
                    mm = pe.matmul(LOG[:, n % 2, m * nk:(m + 1) * nk],
                                   S[r, h // 2, qt * P:(qt + 1) * P], IKT[r, 0:nk],
                                   start=True, stop=True, skip_group_check=True)
                mm.then_inc(idx_ready, 1)

            def tick1(n):
                if n == 2:
                    bias_tables()
                if n == 3:
                    transposes([(EA, EB)[b // 2][:, (b % 2) * P:(b % 2 + 1) * P] for b in range(4)],
                               (psum_free, 1), once["va_transposed"], (once["va_taken"], 1))
                if n == 5:
                    pe.wait_ge(once["ksq1"], 1)
                    pe.wait_ge(rows_copied, 1)
                    pe.matmul(LOG[:, 0, 0:T], ones[0:HD, :], KSQ1[0:HD, :], start=True, stop=True)\
                      .then_inc(once["ksq1_summed"], 1)
                if n - L1_INDEX - 1 in range(12):
                    index(n - L1_INDEX - 1)
                if n == L1_QUERIES + 2:
                    pe.wait_ge(once["q1_squared"], 1)
                    pe.wait_ge(idx_free, 12)
                    for qt in range(2):
                        for t in range(HALF):
                            c = DSA_HEADS * qt + 2 * t
                            mm = pe.matmul(LOG[:, 1, c:c + 2], SQ1[:, t, qt * P:(qt + 1) * P], pair[:, :],
                                           start=True, stop=True, skip_group_check=True)
                    mm.then_inc(once["q1_summed"], 1)
                if n == DSA.at[0]:
                    pe.wait_ge(once["dsa_operands"], 1)
                attend(DSA, n, half_rows(lambda h: HALF + h // 2),
                       lambda h, nk: KT1[HD * (h % 2):HD * (h % 2) + HD, 0:nk],
                       lambda h, kt: V1[:, kt, HD:2 * HD])

            for b in range(10):
                gemm(HH, HL, tick=lambda j: tick1(8 * b + j))
            for half in range(2):
                ps = open_block()
                pe.wait_ge(once["pooled_lo"], 1)
                slot = take_sub()
                wh = WH[:, slot].rearrange("p (g k n) -> p g k n", g=2, k=2)
                wl = WL[:, slot].rearrange("p (g k n) -> p g k n", g=2, k=2)
                for g in range(2):
                    for k in range(2):
                        for n in range(2):
                            c = slice(n * P, (n + 1) * P)
                            kt = 4 * half + 2 * g + k
                            mm = three(ps[:, 2 * g + n], wh[:, g, k, c], wl[:, g, k, c], GH[:, kt], GL[:, kt],
                                       start=(k == 0 and n == 0), stop=(k == 1))
                mm.then_inc(subs_used, 1)
                sub.add()
                tick1(L1_POOL + half)
            gemm_pair(GH, GL, L1_OUT_TILES, (2, 4, 5, 6), lambda n: tick1(L1_POOL + 2 + n))
            gemms(1, GH, GL)

            gemm(HH, HL, ready=(hl_ready, 4))
            ssq(1)

            def tick2(n):
                if n == 3:
                    transposes([KV2[:, 2 + b % 2, (b // 2) * P:(b // 2 + 1) * P] for b in range(4)],
                               (psum_free, L1_BLOCKS + 1), once["v2_transposed"], (once["v2_taken"], 1))
                if n == 4:
                    pe.wait_ge(once["ksq2"], 1)
                    pe.wait_ge(log_free, BEFORE[SWA][1])
                    for a in range(2):
                        r = slice(HD * a, HD * a + HD)
                        mm = pe.matmul(LOG[r, 0, :].rearrange("p (a t) -> p a t", a=2), ones[r, 0:HD],
                                       KSQ2[r, :, :], start=True, stop=True, skip_group_check=True)
                    mm.then_inc(once["ksq2_summed"], 1)
                if n in L2_START:
                    pe.wait_ge(kv_head_ready, L2_START.index(n) + 1)
                attend(SWA, n, half_rows(lambda h: h // 2),
                       lambda h, nk: K2[HD * (h % 2):HD * (h % 2) + HD, h // 8, 0:nk],
                       lambda h, kt: V2[:, kt, h // 16, HD * (h // 8 % 2):HD * (h // 8 % 2) + HD])
                if n in L2_SUMS:
                    j = L2_SUMS.index(n)
                    pe.wait_ge(q2_squared, j + 1)
                    pe.wait_ge(*pt_free[0])
                    for qt in range(2):
                        for t in range(4):
                            c = 8 * qt + 2 * t
                            mm = pe.matmul(PT[:, 0, c:c + 2], SQ2[:, t, qt * P:(qt + 1) * P], pair[:, :],
                                           start=True, stop=True, skip_group_check=True)
                    mm.then_inc(q2_summed, 1)
                    pt_free[0] = (q2_taken, j + 1)

            for b in range(8):
                gemm(HH, HL, tick=lambda j: tick2(8 * b + j))
            gemm_pair(GH, GL, range(NT), (8, 10, 12, 14), lambda n: tick2(64 + n))
            gemms(1, GH, GL)

            for b in range(2):
                gemm(HH, HL, ready=(hl_ready, 8))
                if b == 0:
                    ssq(2)
            gemms(2, HH, HL)

            def tick3(n):
                if n < 4:
                    transposes([V3T[:, 4 * (n // 2) + t, (n % 2) * P:(n % 2 + 1) * P] for t in range(4)],
                               (psum_free, L2_BLOCKS + 2), once[f"v3_transposed{n}"], (once[f"v3_taken{n}"], 1))
                if n == MOBA.at[0]:
                    pe.wait_ge(psum_free, L2_BLOCKS + 6)
                attend(MOBA, n, lambda h, qt: S[:, h, qt * P:(qt + 1) * P],
                       lambda h, nk: S[:, HALF + h, 0:nk], lambda h, kt: V3[:, kt, h, :])

            def lru_gates(half):
                if half == 0:
                    pe.wait_ge(once["xc_lo"], 1)
                    pe.wait_ge(log_free, BEFORE[MOBA][1] + MOBA.n_banks(4))
                    pe.wait_ge(*pt_free[0])
                else:
                    pe.wait_ge(once["lru_taken"], 1)
                slot = take_sub()
                for gate in range(2):
                    for n in range(4):
                        c = slice((4 * gate + n) * P, (4 * gate + n + 1) * P)
                        mm = three(gate_sums(gate, n), WH[:, slot, c], WL[:, slot, c], XCH[:, 4 * half + n],
                                   XCL[:, 4 * half + n], start=(n % 2 == 0), stop=True)
                mm.then_inc(subs_used, 1)
                sub.add()

            for b in range(10):
                gemm(HH, HL, tick=lambda j: tick3(8 * b + j))
                if 8 * b + 8 >= L3_GATES and 8 * b + 8 < L3_GATES + 16:
                    lru_gates((8 * b + 8 - L3_GATES) // 8)
            for BH, BL, k0, ready in ((GH, GL, 0, (gl_ready, 18)), (GH, GL, HALF, (gl_ready, 19)),
                                      (SCH, SCL, 0, (once["sc_lo1"], 1))):
                pe.wait_ge(*ready)
                with loop(pe, 2, [(sub, 6 * AHEAD), (blk, 4)]):
                    for _ in range(2):
                        gemm(HH, HL)
                        gemm(BH, BL, nkt=HALF, k0=k0)
            gemm(GH, GL, ready=(gl_ready, 19))
            gemm(GH, GL)
            gemms(1, GH, GL)

            gemm(HH, HL, ready=(hl_ready, 12))
            ssq(3)
            gemm(HH, HL)
            gemms(1, HH, HL)
            for g in range(4):
                if g:
                    gemms(2, HH, HL)
                gemm(GH, GL, ready=(gl_ready, 23 + 4 * g))
                gemm(GH, GL)
                gemms(1, GH, GL)
            pe.wait_ge(sq_ready, 5)
            for k in range(6):
                if k == 2:
                    pe.wait_ge(once["last_squares"], 1)
                src = SQACC[:, k, :] if k < 2 else LAST_SQ[:, k - 2, :]
                mm = pe.matmul(OP[:, 0:T], ones[:, :], src, start=(k == 0), stop=(k == 5))
            mm.then_inc(ssq_done, 1)

        @block.scalar
        def _(act):
            sub, blk = Count(hi_ready), Count(psum_free)
            raw = [Count(raw_full[k]) for k in range(AHEAD)]
            gr, var, mix, hidden = Count(gate_ready), Count(var_ready), Count(mix_ready), Count(hidden_ready)
            rounds = [(sub, 16), (blk, 2)] + [(c, 16 * 4) for c in raw]

            def splits(n, tick=None):
                for j in range(n):
                    slot = sub.base % AHEAD
                    act.wait_ge(raw_full[slot], raw[slot].add(16))
                    if sub.i is not None or sub.base >= AHEAD:
                        act.wait_ge(subs_used, sub.value - (AHEAD - 1))
                    act.activation(WH[:, slot], RAW[:, slot], ACT.Copy).then_inc(hi_ready, 1)
                    sub.add()
                    if tick:
                        tick(j)

            def block_splits(tick=None):
                splits(8, tick)
                blk.add()

            def root(src, dst):
                act.wait_ge(var_ready, var.add())
                act.activation(dst, src, ACT.Sqrt).then_inc(std_ready, 1)

            def token_root():
                root(TF[:, 0:T], TF[:, T:])

            def h_hi(gain, t0, ready):
                act.wait_ge(*ready)
                for k in range(4):
                    ins = act.activation(HH[:, bass.ds(t0 + k, 1), :], X[:, bass.ds(t0 + k, 1), :], ACT.Copy,
                                         scale=small[:, bass.ds(t0 + (SMALL[gain] + k), 1)])
                ins.then_inc(hh_ready, 1)

            def paired_residual_blocks(gain, tick):
                splits(14, tick)
                for b in range(4):
                    if b:
                        splits(2 if b == 1 else 8)
                    blk.add()
                    h_hi(gain, 4 * b, (psum_free, blk.value))

            def residual_blocks(gain):
                with loop(act, 2, rounds) as i:
                    for b in range(2):
                        block_splits()
                        h_hi(gain, 8 * i + 4 * b, (psum_free, blk.value))

            def attend(a, tick):
                u0, _, pk0, f0 = BEFORE[a]
                L = LBUF[a]
                for u, d, flush in a.due(tick):
                    chunk, qt, _ = a.units[u]
                    pk, fl = pk0 + a.n_packs(u), f0 + a.n_flushes(u)
                    if d == 3:
                        nk = P * (qt + 1)
                        act.wait_ge(max_ready, u0 + u + 1)
                        c = 4 * (chunk % a.per)
                        if a is SWA:
                            act.activation(sink_e[:, fl % 2, c:c + 4], sink_d[:, u % 4, :], ACT.Exp)
                        for h in range(4):
                            ins = act.activation(L[:, u % 2, h, 0:nk], L[:, u % 2, h, 0:nk], ACT.Exp,
                                                 bias=neg_max[:, u % 4, h:h + 1],
                                                 accum_out=sums[:, fl % 2, c + h:c + h + 1])
                        ins.then_inc(p_ready, 1)
                    if d - 5 in range(len(a.packs(u))):
                        k = pk + d - 5
                        act.wait_ge(pt_ready, k + 1)
                        if k >= 2:
                            act.wait_ge(pv_done, k - 1)
                        act.activation(pts[:, k % 2, :].rearrange("p (b q) -> p b q", b=4), PT[:, :, :],
                                       ACT.Copy).then_inc(pt_taken, 1)
                    if flush == 3:
                        t0 = 4 * (a.n_flushes(u) // 2) + (HALF if a is DSA else 0)
                        act.wait_ge(ot_taken, fl + 1)
                        act.activation(GH[:, t0:t0 + 4, qt * P:(qt + 1) * P],
                                       TF[:, :].rearrange("p (b q) -> p b q", b=4), ACT.Copy).then_inc(gh_ready, 1)

            act.dma_start(small[:, :], small_in_dram).then_inc(small_in, 16)
            for n in range(4):
                act.dma_start(X[:, 4 * n:4 * n + 4, :], x_in[:, 4 * n:4 * n + 4, :]).then_inc(x_in_sem[n], 16)
            act.dma_start(TABS[:, :], tables_in).then_inc(consts_in, 16)
            act.dma_start(ONEHOT[:, :, :], onehot_in).then_inc(consts_in, 16)
            act.dma_start(ident[:, :], const_in[:, 0:P]).then_inc(consts_in, 16)
            act.dma_start(INV[:, :, :], const_in[:, P:P + 64].rearrange("p (g t) -> p g t", g=4))\
               .then_inc(consts_in, 16)
            act.wait_ge(small_in, 16)
            for n in range(4):
                t = slice(4 * n, 4 * n + 4)
                h_hi("g_even", 4 * n, (x_in_sem[n], 16))
                splits(1)
                act.activation(S[:, 16 + 4 * n:20 + 4 * n, :], X[:, t, :], ACT.Square).then_inc(sq0_ready, 1)

            splits(4)
            blk.add()
            token_root()

            def tick1(n):
                if n == 2:
                    act.wait_ge(psum_free, 1)
                    act.activation(KSQ1[0:HD, :], EA[0:HD, :], ACT.Square).then_inc(once["ksq1"], 1)
                if n == 6:
                    root(TF[:, 0:T], TF[:, T:])
                if n - L1_INDEX - 1 in range(12):
                    k = n - L1_INDEX - 1
                    act.wait_ge(idx_ready, k + 1)
                    if k >= 2:
                        act.wait_ge(relu_used, k - 1)
                    act.activation(RELU[:, k % 2, :], LOG[:, k % 2, :], ACT.Relu).then_inc(idx_free, 1)
                if n == L1_QUERIES:
                    act.wait_ge(psum_free, 5)
                    act.activation(SQ1[:, :, :], S[:, HALF:2 * HALF, :], ACT.Square).then_inc(once["q1_squared"], 1)
                if n == L1_QUERIES + 4:
                    root(TF[:, 0:32], TF[:, T:T + 32])
                if n == L1_ATTEND + 16:
                    act.wait_ge(psum_free, 9)
                    act.activation(S[:, 16:24, :], S[:, 16:24, :], ACT.Silu).then_inc(once["silu1"], 1)
                attend(DSA, n)
                if n == L1_POOL - 5:
                    act.wait_ge(once["pooled"], 1)
                    act.activation(GH[:, 0:8, :], S[:, 0:8, :], ACT.Copy).then_inc(once["pooled_hi"], 1)
                if n in (L1_POOL - 8, L1_POOL):
                    half = n // L1_POOL
                    act.wait_ge(psum_free, L1_PROJ - 1 + half)
                    g = S[:, 32 + 4 * half:36 + 4 * half, :]
                    act.activation(g, g, ACT.Silu).then_inc(once["silu_pool"], 1)

            for b in range(10):
                block_splits(lambda j: tick1(8 * b + j))
            for half in range(2):
                splits(1, lambda j: tick1(L1_POOL + half))
                blk.add()
                act.wait_ge(psum_free, blk.value)
                act.activation(GH[:, 4 * half:4 * half + 4, :], S[:, 24 + 4 * half:28 + 4 * half, :], ACT.Copy)\
                   .then_inc(gh_ready, 1)
            paired_residual_blocks("g_odd", lambda j: tick1(L1_POOL + 2 + j))

            block_splits()
            token_root()

            def tick2(n):
                if n == 2:
                    act.wait_ge(psum_free, L1_BLOCKS + 1)
                    act.activation(KSQ2[:, :, :], KV2[:, 0:2, :], ACT.Square).then_inc(once["ksq2"], 1)
                if n == 5:
                    root(TF[:, :].rearrange("p (a t) -> p a t", a=2), o_sb[:, :].rearrange("p (a t) -> p a t", a=2))
                if n + 2 in L2_SUMS:
                    j = L2_SUMS.index(n + 2)
                    act.wait_ge(psum_free, L1_BLOCKS + 2 + L2_ORDER.index(f"q{j}"))
                    if j:
                        act.wait_ge(q2_summed, j)
                    act.activation(SQ2[:, :, :], S[:, 4 * j:4 * j + 4, :], ACT.Square).then_inc(q2_squared, 1)
                attend(SWA, n)
                if n in (25, 41, 57, 65):
                    act.wait_ge(psum_free, L1_BLOCKS + 1 + n // 8)
                    j = int(L2_ORDER[n // 8 - 1][1])
                    g = S[:, 16 + 4 * j:20 + 4 * j, :]
                    act.activation(g, g, ACT.Silu).then_inc(silu2, 1)
                if n - 1 in L2_SUMS:
                    root(q_var[:, 0, :], q_var[:, 1, :])

            for b in range(8):
                block_splits(lambda j: tick2(8 * b + j))
            paired_residual_blocks("g_mix", lambda j: tick2(64 + j))

            block_splits()
            token_root()
            block_splits()
            with loop(act, 2, rounds):
                for _ in range(2):
                    block_splits()

            def lru_sigmoids(gate, half):
                dst, b = ((LRU_M, "ba"), (LRU_I, "bx"))[gate]
                for n in range(4):
                    t = 4 * half + n
                    ins = act.activation(dst[:, t, :], gate_sums(gate, n), ACT.Sigmoid, bias=col(b, t))
                return ins

            def sc_hi(half):
                act.wait_ge(once[f"sc_ready{half}"], 1)
                t = slice(4 * half, 4 * half + 4)
                act.activation(SCH[:, t, :], S[:, 48 + 4 * half:52 + 4 * half, :], ACT.Copy)\
                   .then_inc(once[f"sc_hi{half}"], 1)

            def tick3(n):
                attend(MOBA, n)
                if n == L3_CONV + 16:
                    act.wait_ge(once["xc_ready"], 1)
                    act.activation(XCH[:, :, :], XC, ACT.Copy).then_inc(once["xc_hi"], 1)
                if n == L3_CONV + 17:
                    act.wait_ge(once["abs_lam"], 1)
                    act.activation(SP8[:, 1, :], SP8[:, 0, :], ACT.Exp, scale=-1.0).then_inc(once["exp_lam"], 1)
                if n == L3_GATES:
                    act.wait_ge(subs_used, lru_subs[0])
                    lru_sigmoids(0, 0)
                if n == L3_GATES + 1:
                    lru_sigmoids(1, 0).then_inc(once["lru_taken"], 1)
                if n == L3_GATES + 8:
                    act.wait_ge(subs_used, lru_subs[1])
                    lru_sigmoids(0, 1)
                if n == L3_GATES + 9:
                    lru_sigmoids(1, 1).then_inc(act_step, 1)
                    act.wait_ge(act_step, 1)
                    act.wait_ge(once["sp_ready"], 1)
                if n in (L3_LRU - 1, L3_LRU):
                    for t in range(4 * (n - L3_LRU + 1), 4 * (n - L3_LRU + 2)):
                        ins = act.activation(LRU_A[:, t, :], LRU_M[:, t, :], ACT.Exp, scale=SP8[:, 6, t:t + 1])
                    if n == L3_LRU:
                        ins.then_inc(once["decays"], 1)
                        act.wait_ge(once["decays"], 1)
                if n == L3_LRU + 1:
                    for t in range(HALF):
                        act.activation(LRU_M[:, t, :], LRU_M[:, t, :], ACT.Tanh, scale=SP8[:, 7, t:t + 1])
                if n == L3_LRU + 2:
                    act.activation(LRU_A2[:, :, :], LRU_A[:, :, :], ACT.Square).then_inc(once["a_squared"], 1)
                if n == L3_LRU + 4:
                    act.wait_ge(once["m2_ready"], 1)
                    act.activation(LRU_M, LRU_M, ACT.Sqrt, scale=2.0 ** 100).then_inc(once["mult_ready"], 1)
                if n == L3_LRU + 6:
                    act.wait_ge(psum_free, L3_BLOCKS - 2)
                    act.activation(S[:, 32:40, :], S[:, 32:40, :], ACT.Gelu_apprx_tanh)\
                       .then_inc(once["gelu_ready"], 1)
                if n == L3_LRU + 17:
                    act.wait_ge(once["lru_ready"], 1)
                    act.activation(GH[:, 8:16, :], S[:, 32:40, :], ACT.Copy).then_inc(gh_ready, 1)
                if n == 74:
                    sc_hi(0)

            lru_subs = []
            for b in range(10):
                block_splits(lambda j: tick3(8 * b + j))
                if 8 * b + 8 in (L3_GATES, L3_GATES + 8):
                    splits(1)
                    lru_subs.append(sub.base - AHEAD)
            sc_hi(1)
            for branch in range(3):
                last = branch == 2
                steps = [(sub, 24), (blk, 4)] + [(c, 16 * 6) for c in raw] + [(mix, 2)] * last
                with loop(act, 2, steps) as i:
                    for b in range(2):
                        block_splits()
                        act.wait_ge(psum_free, blk.value)
                        for k in range(4):
                            t = 8 * i + (4 * b + k + SMALL["gate_b"] + NT * branch)
                            ins = act.activation(SG[:, k, :], MT[:, k, :], ACT.Sigmoid,
                                                 bias=small[:, bass.ds(t, 1)])
                        ins.then_inc(gate_ready, 1)
                        splits(4)
                        blk.add()
                        if last:
                            t = bass.ds(8 * i + 4 * b, 4)
                            act.wait_ge(mix_ready, mix.add())
                            act.activation(GH[:, t, :], MIX[:, t, :], ACT.Copy).then_inc(gh_ready, 1)
            residual_blocks("g_mlp")

            def hidden_hi(t0):
                act.wait_ge(hidden_ready, hidden.add())
                act.activation(GH[:, bass.ds(t0, 4), :], UU, ACT.Copy).then_inc(gh_ready, 1)

            for g in range(4):
                if g == 0:
                    block_splits()
                    token_root()
                    hidden_hi(0)
                    for b in range(1, 4):
                        block_splits()
                        hidden_hi(4 * b)
                else:
                    with loop(act, 2, rounds + [(hidden, 2)]) as i:
                        for b in range(2):
                            block_splits()
                            hidden_hi(8 * i + 4 * b)
                if g < 3:
                    with loop(act, 2, rounds):
                        for _ in range(2):
                            block_splits()
            splits(n_subs - sub.base)
            blk.add(4)
            act.wait_ge(psum_free, blk.value)
            act.activation(LAST_SQ, X[:, 12:16, :], ACT.Square).then_inc(once["last_squares"], 1)
            token_root()

        @block.vector
        def _(dve):
            sub, used, blk = Count(lo_ready), Count(subs_used), Count(psum_free)
            hh, gh, gr, steps_n = Count(hh_ready), Count(gh_ready), Count(gate_ready), Count(dve_step)
            std = Count(std_ready)
            rounds = [(sub, 16), (used, 16), (blk, 2)]

            def splits(n, tick=None):
                for j in range(n):
                    slot = sub.base % AHEAD
                    dve.wait_ge(hi_ready, sub.value + 1)
                    dve.tensor_tensor(WL[:, slot], RAW[:, slot], WH[:, slot].bitcast(F32), ALU.subtract)\
                       .then_inc(lo_ready, 1)
                    sub.add()
                    if tick:
                        tick(j)

            def step(ins):
                ins.then_inc(dve_step, 1)
                dve.wait_ge(dve_step, steps_n.add())

            def block_done(n=8):
                dve.wait_ge(subs_used, used.add(n))
                blk.add()
                return GP[:, (blk.base - 1) % 2]

            def rs_of(n):
                return rs[:, None, :].to_broadcast([P, n, T])

            def times_rs(dst):
                ps = block_done()
                for k in (0, 2):
                    ins = dve.tensor_tensor(dst(k), ps[:, k:k + 2], rs_of(2), ALU.mult)
                ins.then_inc(psum_free, 1)

            def variance(src, n, var, ready):
                dve.wait_ge(*ready)
                return dve.tensor_scalar(var, src, 1.0 / n, EPS, ALU.mult, ALU.add).then_inc(var_ready, 1)

            def rsqrt_of(var, tmp, y):
                dve.wait_ge(std_ready, std.add())
                step(dve.reciprocal(y, tmp))
                step(dve.tensor_tensor(tmp, y, y, ALU.mult))
                step(dve.tensor_tensor(tmp, tmp, var, ALU.mult))
                step(dve.tensor_scalar(tmp, tmp, -0.5, 1.5, ALU.mult, ALU.add))
                step(dve.tensor_tensor(y, y, tmp, ALU.mult))

            def rsqrt(src, n, var, tmp, y, ready):
                variance(src, n, var, ready)
                rsqrt_of(var, tmp, y)

            def token_norm(n):
                rsqrt(OP[:, 0:T], D, TF[:, 0:T], TF[:, T:], rs[:, :], (ssq_done, n + 1))

            def h_lo(gain, t0):
                dve.wait_ge(hh_ready, hh.add())
                for k in range(4):
                    s = bass.ds(t0 + k, 1)
                    ins = dve.scalar_tensor_tensor(out=HL[:, s, :], in0=X[:, s, :],
                                                   scalar=small[:, bass.ds(t0 + (SMALL[gain] + k), 1)],
                                                   in1=HH[:, s, :].bitcast(F32), op0=ALU.mult, op1=ALU.subtract)
                ins.then_inc(hl_ready, 1)

            def g_lo(dst, src, hi):
                dve.wait_ge(gh_ready, gh.add())
                dve.tensor_tensor(dst, src, hi.bitcast(F32), ALU.subtract).then_inc(gl_ready, 1)

            def add_residual(t0, subs=8):
                ps = block_done(subs)
                for k in (0, 2):
                    s = bass.ds(t0 + k, 2)
                    ins = dve.tensor_tensor(X[:, s, :], ps[:, k:k + 2], X[:, s, :], ALU.add)
                ins.then_inc(psum_free, 1)

            def paired_residual_blocks(gain, tick):
                splits(14, tick)
                for b in range(4):
                    if b:
                        splits(2 if b == 1 else 8)
                    add_residual(4 * b, (14, 2, 8, 8)[b])
                    h_lo(gain, 4 * b)

            def residual_blocks(gain):
                with loop(dve, 2, rounds + [(hh, 2)]) as i:
                    for b in range(2):
                        splits(8)
                        add_residual(8 * i + 4 * b)
                        h_lo(gain, 8 * i + 4 * b)

            def attend(a, tick, scale, gate=True, mask=None):
                u0, bank0, pk0, f0 = BEFORE[a]
                L, B = LBUF[a], BBUF[a]
                for u, d, flush in a.due(tick):
                    chunk, qt, _ = a.units[u]
                    bank, fl = bank0 + a.n_banks(u), f0 + a.n_flushes(u)
                    if d == 1:
                        nk, gc = P * (qt + 1), a.row0 // 4 + chunk
                        if qt:
                            dve.wait_ge(bias_in[gc % 2], 16 * (gc // 2 + 1))
                        if u >= 2:
                            dve.wait_ge(pt_ready, pk0 + a.n_packs(u - 1))
                        for heads in a.banks(u):
                            dve.wait_ge(log_ready, bank + 1)
                            for m, h in enumerate(heads):
                                ins = dve.scalar_tensor_tensor(
                                    out=L[:, u % 2, h, 0:nk], in0=LOG[:, bank % 2, m * nk:(m + 1) * nk],
                                    scalar=scale(4 * chunk + h, qt), in1=B[:, gc % 2, h, T - nk:T],
                                    op0=ALU.mult, op1=ALU.add)
                            ins.then_inc(log_free, 1)
                            bank += 1
                        dve.wait_ge(log_free, bank)
                        if mask is not None:
                            step(dve.tensor_tensor(L[:, u % 2, :, 0:nk], L[:, u % 2, :, 0:nk],
                                                   mask(qt)[:, None, :].to_broadcast([P, 4, nk]), ALU.add))
                        nm = neg_max[:, u % 4, :]
                        ins = dve.tensor_reduce(nm, L[:, u % 2, :, 0:nk], AX_X, ALU.max, negate=True)
                        if a is SWA:
                            step(ins)
                            sink = col("sinks", 4 * chunk, 4)
                            step(dve.scalar_tensor_tensor(out=nm, in0=sink, scalar=-1.0, in1=nm,
                                                          op0=ALU.mult, op1=ALU.min))
                            ins = dve.tensor_tensor(sink_d[:, u % 4, :], sink, nm, ALU.add)
                        ins.then_inc(max_ready, 1)
                    t0 = 4 * (a.n_flushes(u) // 2) + (HALF if a is DSA else 0)
                    tf = TF[:, :].rearrange("p (b q) -> p b q", b=4)
                    q = slice(qt * P, (qt + 1) * P)
                    if flush == 0:
                        n = 4 * a.per
                        dve.wait_ge(p_ready, u0 + u + 1)
                        if a is SWA:
                            step(dve.tensor_tensor(sums[:, fl % 2, 0:n], sums[:, fl % 2, 0:n],
                                                   sink_e[:, fl % 2, 0:n], ALU.add))
                        step(dve.reciprocal(r_sums[:, 0:n], sums[:, fl % 2, 0:n]))
                        dve.wait_ge(pv_done, pk0 + a.n_packs(u + 1))
                        if fl:
                            dve.wait_ge(ot_ready, fl)
                        dve.tensor_tensor(o_sb[:, :].rearrange("p (h d) -> p h d", h=n),
                                          OP[:, :].rearrange("p (h d) -> p h d", h=n),
                                          r_sums[:, 0:n, None].to_broadcast([P, n, a.hd]), ALU.mult)\
                           .then_inc(o_ready, 1)
                    if flush == 3:
                        dve.wait_ge(ot_ready, fl + 1)
                        if gate:
                            g = 4 * (a.n_flushes(u) // 2)
                            ins = dve.tensor_tensor(tf, PT[:, :, :], S[:, 16 + g:20 + g, q], ALU.mult)
                        else:
                            ins = dve.tensor_copy(tf, PT[:, :, :])
                        ins.then_inc(ot_taken, 1)
                    if flush == 4:
                        g_lo(GL[:, t0:t0 + 4, q], tf, GH[:, t0:t0 + 4, q])

            for n in range(4):
                h_lo("g_even", 4 * n)
                splits(1)
            dve.wait_ge(sq0_ready, 4)
            for k in (16, 24):
                step(dve.tensor_tensor(S[:, k:k + 4, :], S[:, k:k + 4, :], S[:, k + 4:k + 8, :], ALU.add))
            step(dve.tensor_tensor(S[:, 16:20, :], S[:, 16:20, :], S[:, 24:28, :], ALU.add))
            dve.tensor_tensor(SQACC[:, :, :], S[:, 16:18, :], S[:, 18:20, :], ALU.add).then_inc(sq_ready, 1)
            dve.wait_ge(small_in, 16)
            dve.tensor_tensor(gg[:, 0:1], col("dsa_q"), col("dsa_k"), ALU.mult)
            step(dve.tensor_tensor(gg[:, 1:2], col("swa_q"), col("swa_k"), ALU.mult))

            splits(4)
            token_norm(0)
            ps = block_done(4)
            dve.tensor_tensor(S[:, 40:42, :], ps[:, 0:2], rs_of(2), ALU.mult)
            for a in range(2):
                ins = dve.tensor_tensor(IKT[HD * a:HD * a + HD, :], ps[0:HD, 1], rs[0:HD, :], ALU.mult)
            ins.then_inc(psum_free, 1)

            def scores(n):
                qt, heads = [(qt, heads) for qt in (1, 0) for heads in index_banks(qt)][n]
                nk, at = P * (qt + 1), 0 if qt else T
                score = SCORE[:, at:at + nk]
                dve.wait_ge(idx_free, n + 1)
                for m, h in enumerate(heads):
                    w = IW[:, qt, HD + h:HD + h + 1]
                    relu = RELU[:, n % 2, m * nk:(m + 1) * nk]
                    if h == 0:
                        step(dve.tensor_scalar(score, relu, w, None, ALU.mult))
                    else:
                        step(dve.scalar_tensor_tensor(out=score, in0=relu, scalar=w, in1=score,
                                                      op0=ALU.mult, op1=ALU.add))
                dve.sem_inc(relu_used, 1)

            def tick1(n):
                if n == 3:
                    dve.wait_ge(rows_done, 1)
                    dve.tensor_copy(ROWS_SB[:, 0:2, :], LOG[0:32, :, 0:ROWS])
                    dve.tensor_copy(ROWS_SB[:, 2, :], OP[0:32, 0:ROWS]).then_inc(rows_copied, 1)
                if n == 4:
                    dve.wait_ge(once["va_transposed"], 1)
                    dve.tensor_copy(V1[:, :, :], PT[:, 0:2, :])
                    dve.tensor_scalar(IW[:, :, :], PT[:, 2:4, :], DSA_HEADS ** -0.5 * HD ** -0.5, None, ALU.mult)\
                       .then_inc(once["va_taken"], 1)
                if n == 6:
                    rsqrt(LOG[:, 0, 0:T], HD, TF[:, 0:T], TF[:, T:], RK1[:, :], (once["ksq1_summed"], 1))
                    for a in range(2):
                        ins = dve.scalar_tensor_tensor(out=KT1[HD * a:HD * a + HD, :], in0=EA[0:HD, :],
                                                       scalar=gg[0:HD, 0:1], in1=RK1[0:HD, :], op0=ALU.mult,
                                                       op1=ALU.mult)
                    step(ins)
                    dve.wait_ge(once["va_taken"], 1)
                if n - L1_INDEX - 2 in range(12):
                    scores(n - L1_INDEX - 2)
                if n == L1_INDEX + 14:
                    dve.sem_inc(score_ready, 1)
                if n == L1_QUERIES + 4:
                    rsqrt(LOG[:, 1, 0:32], HD, TF[:, 0:32], TF[:, T:T + 32], rq[:, 0:32], (once["q1_summed"], 1))
                    step(dve.tensor_scalar(rq[:, 0:32], rq[:, 0:32], HD ** -0.5, None, ALU.mult))
                if n - L1_QUERIES in range(TOPK // 4):
                    if n == L1_QUERIES:
                        dve.wait_ge(score_causal, 1)
                    qt = n % 2
                    score = SCORE[:, T * (1 - qt):T * (1 - qt) + P * (qt + 1)]
                    step(dve.max(TOP8[:, qt, :], score))
                    step(dve.match_replace(score, TOP8[:, qt, :], score, TAKEN))
                if n == L1_ATTEND:
                    step(dve.tensor_scalar(SCORE[:, :], SCORE[:, :], 0.5 * (TAKEN + FUTURE), NEG, ALU.is_gt,
                                           ALU.mult))
                    dve.sem_inc(once["dsa_operands"], 1)
                if n == DSA.at[1] + 10:
                    dve.wait_ge(once["silu1"], 1)
                attend(DSA, n, lambda h, qt: rq[:, 16 * qt + h:16 * qt + h + 1],
                       mask=lambda qt: SCORE[:, 0:T] if qt else SCORE[:, T:])
                if n == L1_POOL - 4:
                    dve.wait_ge(once["pooled_hi"], 1)
                    dve.tensor_tensor(GL[:, 0:8, :], S[:, 0:8, :], GH[:, 0:8, :].bitcast(F32), ALU.subtract)\
                       .then_inc(once["pooled_lo"], 1)

            for b in range(10):
                splits(8, lambda j: tick1(8 * b + j))
                t0 = 8 * (0, 1, 3, 2, 4)[b // 2] + 4 * (b % 2)
                times_rs(lambda k: S[:, t0 + k:t0 + k + 2, :])
            for half in range(2):
                splits(1, lambda j: tick1(L1_POOL + half))
                ps = block_done(1)
                dve.wait_ge(once["silu_pool"], half + 1)
                for k in range(4):
                    t = 4 * half + k
                    ins = dve.scalar_tensor_tensor(out=S[:, 24 + t, :], in0=ps[:, k], scalar=col("pool_scale", t),
                                                   in1=S[:, 32 + t, :], op0=ALU.mult, op1=ALU.mult)
                ins.then_inc(psum_free, 1)
                t = slice(4 * half, 4 * half + 4)
                g_lo(GL[:, t, :], S[:, 24 + 4 * half:28 + 4 * half, :], GH[:, t, :])
            paired_residual_blocks("g_odd", lambda j: tick1(L1_POOL + 2 + j))

            splits(8)
            token_norm(1)
            times_rs(lambda k: KV2[:, k:k + 2, :])

            def tick2(n):
                if n == 3:
                    dve.wait_ge(once["v2_transposed"], 1)
                    dve.tensor_copy(V2[:, :, :, :].rearrange("p a b c -> p (a b) c"), PT[:, :, :])\
                       .then_inc(once["v2_taken"], 1)
                if n == 5:
                    rsqrt(LOG[:, 0, :].rearrange("p (a t) -> p a t", a=2), HD,
                          TF[:, :].rearrange("p (a t) -> p a t", a=2),
                          o_sb[:, :].rearrange("p (a t) -> p a t", a=2), RK2[:, :, :], (once["ksq2_summed"], 1))
                if n in (6, 9, 12, 13):
                    k = (6, 9, 12, 13).index(n)
                    r = slice(HD * (k % 2), HD * (k % 2) + HD)
                    for a in range(2):
                        step(dve.scalar_tensor_tensor(out=K2[HD * a:HD * a + HD, k, :], in0=KV2[r, k // 2, :],
                                                      scalar=gg[r, 1:2], in1=RK2[r, k // 2, :], op0=ALU.mult,
                                                      op1=ALU.mult))
                    dve.sem_inc(kv_head_ready, 1)
                for j in range(4):
                    if n == SWA.at[4 * j + 1] + 10:
                        dve.wait_ge(silu2, j + 1)
                if n - 1 in L2_SUMS:
                    j = L2_SUMS.index(n - 1)
                    variance(PT[:, 0, 0:16], HD, q_var[:, 0, :], (q2_summed, j + 1))
                    dve.wait_ge(var_ready, std.base + 1)
                    dve.sem_inc(q2_taken, 1)
                attend(SWA, n, lambda h, qt: rq[:, 16 * (h // 8) + 8 * qt + h % 8:16 * (h // 8) + 8 * qt + h % 8 + 1])
                if n - 2 in L2_SUMS:
                    j = L2_SUMS.index(n - 2)
                    y = rq[:, 16 * j:16 * j + 16]
                    rsqrt_of(q_var[:, 0, :], q_var[:, 1, :], y)
                    step(dve.tensor_scalar(y, y, HD ** -0.5, None, ALU.mult))

            for b in range(8):
                splits(8, lambda j: tick2(8 * b + j))
                t0 = 4 * int(L2_ORDER[b][1]) + (NT if L2_ORDER[b][0] == "g" else 0)
                times_rs(lambda k: S[:, t0 + k:t0 + k + 2, :])
            paired_residual_blocks("g_mix", lambda j: tick2(64 + j))

            for b in range(2):
                splits(8)
                if b == 0:
                    token_norm(2)
                times_rs(lambda k: V3T[:, 4 * b + k:4 * b + k + 2, :])
            with loop(dve, 2, rounds) as i:
                for b in range(2):
                    splits(8)
                    times_rs(lambda k: S[:, bass.ds(8 * i + (4 * b + k), 2), :])

            def taps(dst, src, t, name, n, bias=None):
                w = col(name, HALF * (n - 1) + t)
                if bias is None:
                    ins = dve.tensor_scalar(dst, src, w, None, ALU.mult)
                else:
                    ins = dve.tensor_scalar(dst, src, w, col(bias, t), ALU.mult, ALU.add)
                for d in range(1, n):
                    step(ins)
                    ins = dve.scalar_tensor_tensor(out=dst[:, d:], in0=src[:, 0:T - d],
                                                   scalar=col(name, HALF * (n - 1 - d) + t),
                                                   in1=dst[:, d:], op0=ALU.mult, op1=ALU.add)
                return ins

            def short_conv(t):
                step(dve.tensor_tensor(S[:, 40 + t, :], S[:, 40 + t, :], S[:, 48 + t, :], ALU.mult))
                taps(S[:, 48 + t, :], S[:, 40 + t, :], t, "sc_w", 3)

            def sc_product(half):
                t = slice(48 + 4 * half, 52 + 4 * half)
                dve.wait_ge(psum_free, L3_BLOCKS - 1 + half)
                dve.tensor_tensor(S[:, t, :], S[:, t, :], S[:, 16 + 4 * half:20 + 4 * half, :], ALU.mult)\
                   .then_inc(once[f"sc_ready{half}"], 1)

            def sc_lo(half):
                dve.wait_ge(once[f"sc_hi{half}"], 1)
                t = slice(4 * half, 4 * half + 4)
                dve.tensor_tensor(SCL[:, t, :], S[:, 48 + 4 * half:52 + 4 * half, :], SCH[:, t, :].bitcast(F32),
                                  ALU.subtract).then_inc(once[f"sc_lo{half}"], 1)

            def softplus():
                dve.wait_ge(once["exp_lam"], 1)
                e, y, y2, acc = SP8[:, 1, :], SP8[:, 2, :], SP8[:, 3, :], SP8[:, 4, :]
                step(dve.tensor_scalar(y, e, 2.0, None, ALU.add))
                step(dve.reciprocal(y2, y))
                step(dve.tensor_tensor(y, e, y2, ALU.mult))
                step(dve.tensor_tensor(y2, y, y, ALU.mult))
                step(dve.tensor_scalar(acc, y2, 1.0 / (2 * LN1P_TERMS + 1), None, ALU.mult))
                for k in range(LN1P_TERMS - 1, 0, -1):
                    step(dve.scalar_tensor_tensor(out=acc, in0=acc, scalar=1.0 / (2 * k + 1), in1=y2,
                                                  op0=ALU.add, op1=ALU.mult))
                step(dve.scalar_tensor_tensor(out=acc, in0=acc, scalar=1.0, in1=y, op0=ALU.add, op1=ALU.mult))
                step(dve.tensor_scalar(y, lam, -1.0, 0.0, ALU.mult, ALU.max))
                step(dve.scalar_tensor_tensor(out=acc, in0=acc, scalar=2.0, in1=y, op0=ALU.mult, op1=ALU.add))
                dve.tensor_scalar(SP8[:, 6, :], acc, -8.0, None, ALU.mult)
                dve.tensor_scalar(SP8[:, 7, :], acc, 8.0, None, ALU.mult).then_inc(once["sp_ready"], 1)

            lam = col("lam", 0, HALF)

            def tick3(n):
                if n < 4:
                    dve.wait_ge(once[f"v3_transposed{n}"], 1)
                    dve.tensor_copy(V3[:, n % 2, 4 * (n // 2):4 * (n // 2) + 4, :], PT[:, :, :])\
                       .then_inc(once[f"v3_taken{n}"], 1)
                attend(MOBA, n, lambda h, qt: MHD ** -0.5, gate=False)
                k = n - L3_CONV
                if k in range(0, 16, 2):
                    ins = taps(XC[:, k // 2, :], S[:, 24 + k // 2, :], k // 2, "conv_w", 4, "conv_b")
                    if k == 14:
                        ins.then_inc(once["xc_ready"], 1)
                if k == 17:
                    dve.wait_ge(once["xc_hi"], 1)
                    dve.tensor_tensor(XCL[:, :, :], XC, XCH[:, :, :].bitcast(F32), ALU.subtract)\
                       .then_inc(once["xc_lo"], 1)
                    dve.scalar_tensor_tensor(out=SP8[:, 0, :], in0=lam, scalar=-1.0, in1=lam, op0=ALU.mult,
                                             op1=ALU.max).then_inc(once["abs_lam"], 1)
                if k == 18:
                    softplus()
                k = n - L3_SC
                if k in range(0, 16, 2):
                    short_conv(k // 2)
                if n == 73:
                    sc_product(0)
                if n == 75:
                    sc_lo(0)
                k = n - L3_LRU
                if k == 3:
                    dve.wait_ge(once["a_squared"], 1)
                    dve.scalar_tensor_tensor(out=LRU_M, in0=LRU_A2[:, :, :], scalar=1.0, in1=LRU_M,
                                             op0=ALU.add, op1=ALU.mult).then_inc(once["m2_ready"], 1)
                if k == 5:
                    dve.wait_ge(once["mult_ready"], 1)
                    step(dve.scalar_tensor_tensor(out=LRU_I[:, :, :], in0=LRU_M, scalar=2.0 ** -50,
                                                  in1=LRU_I[:, :, :], op0=ALU.mult, op1=ALU.mult))
                if k == 7:
                    step(dve.tensor_tensor(XC, XC, LRU_I[:, :, :], ALU.mult))
                if k - 8 in range(8):
                    t = k - 8
                    step(dve.tensor_tensor_scan(out=S[:, 24 + t, :], data0=LRU_A[:, t, :], data1=XC[:, t, :],
                                                initial=0.0, op0=ALU.mult, op1=ALU.add))
                if k == 16:
                    dve.wait_ge(once["gelu_ready"], 1)
                    dve.tensor_tensor(S[:, 32:40, :], S[:, 32:40, :], S[:, 24:32, :], ALU.mult)\
                       .then_inc(once["lru_ready"], 1)
                if k == 18:
                    g_lo(GL[:, 8:16, :], S[:, 32:40, :], GH[:, 8:16, :])

            for b, t0 in enumerate(8 * u + 4 * half for u in (3, 5, 6, 4, 2) for half in range(2)):
                splits(8, lambda j: tick3(8 * b + j))
                times_rs(lambda k: S[:, t0 + k:t0 + k + 2, :])
                if 8 * b + 8 in (L3_GATES, L3_GATES + 8):
                    splits(1)
                    used.add(1)
            sc_product(1)
            sc_lo(1)
            for branch in range(3):
                last = branch == 2
                steps = [(sub, 24), (used, 24), (blk, 4), (gr, 2)]
                steps += [(gh, 2)] * last
                with loop(dve, 2, steps) as i:
                    for b in range(2):
                        t0 = 8 * i + 4 * b
                        splits(8)
                        times_rs(lambda k: MT[:, k:k + 2, :])
                        splits(4)
                        ps = block_done(4)
                        dve.wait_ge(gate_ready, gr.add())
                        for k in (0, 2):
                            dst = MT[:, k:k + 2, :] if branch else MIX[:, bass.ds(t0 + k, 2), :]
                            ins = dve.tensor_tensor(dst, ps[:, k:k + 2], SG[:, k:k + 2, :], ALU.mult)
                        ins.then_inc(psum_free, 1)
                        if branch:
                            mix = MIX[:, bass.ds(t0, 4), :]
                            dve.wait_ge(psum_free, blk.value)
                            ins = dve.tensor_tensor(mix, mix, MT[:, :, :], ALU.add)
                            if last:
                                ins.then_inc(mix_ready, 1)
                                g_lo(GL[:, bass.ds(t0, 4), :], mix, GH[:, bass.ds(t0, 4), :])
            residual_blocks("g_mlp")

            def hidden(t0):
                times_rs(lambda k: UT[:, k:k + 2, :])
                dve.wait_ge(psum_free, blk.value)
                dve.scalar_tensor_tensor(out=UU, in0=UT, scalar=0.0, in1=UT, op0=ALU.max, op1=ALU.mult)\
                   .then_inc(hidden_ready, 1)
                g_lo(GL[:, bass.ds(t0, 4), :], UU, GH[:, bass.ds(t0, 4), :])

            for g in range(4):
                if g == 0:
                    splits(8)
                    token_norm(3)
                    hidden(0)
                    for b in range(1, 4):
                        splits(8)
                        hidden(4 * b)
                else:
                    with loop(dve, 2, rounds + [(gh, 2)]) as i:
                        for b in range(2):
                            splits(8)
                            hidden(8 * i + 4 * b)
                if g < 3:
                    with loop(dve, 2, rounds) as i:
                        for b in range(2):
                            splits(8)
                            add_residual(8 * i + 4 * b)
            for b in range(4):
                splits(min(8, n_subs - sub.base))
                add_residual(4 * b)
            token_norm(4)
            for t in range(NT):
                ins = dve.scalar_tensor_tensor(out=S[:, 16 + t, :], in0=X[:, t, :], scalar=col("g_final", t),
                                               in1=rs[:, :], op0=ALU.mult, op1=ALU.mult)
                if t % 4 == 3:
                    ins.then_inc(out_ready, 1)

        @block.gpsimd
        def _(pool):
            steps_n = Count(pool_step)

            def step(ins):
                ins.then_inc(pool_step, 1)
                pool.wait_ge(pool_step, steps_n.add())

            def squares(n, ready, groups=4):
                if n:
                    pool.wait_ge(ssq_done, n)
                for j in range(groups):
                    pool.wait_ge(*ready(j))
                    for k in range(4 * j, 4 * j + 4, 2):
                        x = X[:, k:k + 2, :]
                        if k == 0:
                            step(pool.tensor_tensor(SQACC[:, :, :], x, x, ALU.mult))
                        else:
                            step(pool.tensor_tensor(SQTMP[:, :, :], x, x, ALU.mult))
                            step(pool.tensor_tensor(SQACC[:, :, :], SQACC[:, :, :], SQTMP[:, :, :], ALU.add))
                pool.sem_inc(sq_ready, 1)

            def load_biases(a, chunks):
                for chunk in chunks:
                    gc = a.row0 // 4 + chunk
                    if chunk >= 2:
                        u = a.units.index((chunk - 2, 0, (chunk - 2) % a.per == a.per - 1))
                        pool.wait_ge(log_free, BEFORE[a][1] + a.n_banks(u + 1))
                    elif BEFORE[a][1]:
                        pool.wait_ge(log_free, BEFORE[a][1])
                    src = bass.AP(bias_rows, (a.row0 + 4 * chunk) * bias_head + P - 1,
                                  [[ROWS, P], [bias_head, 4], [1, T]])
                    pool.dma_start(BBUF[a][:, gc % 2], src).then_inc(bias_in[gc % 2], 16)

            step(pool.memset(ones[:, :], 1.0))
            step(pool.memset(pair[:, :], 0.0))
            for a in range(2):
                step(pool.memset(pair[HD * a:HD * a + HD, a:a + 1], 1.0))
            pool.sem_inc(consts_set, 1)
            pool.wait_ge(rows_copied, 1)

            def store_biases(chunks):
                for gc in chunks:
                    pool.wait_ge(subs_used, 10 + 3 * gc)
                    a = MOBA if 4 * gc >= MOBA.row0 else SWA if 4 * gc >= SWA.row0 else DSA
                    r = slice(4 * gc - a.row0, 4 * gc - a.row0 + 4)
                    pool.dma_start(bias_rows.ap()[4 * gc:4 * gc + 4, :, 0:ROWS],
                                   ROWS_SB[r, (DSA, SWA, MOBA).index(a), None, :].to_broadcast([4, P, ROWS]))\
                        .then_inc(rows_stored, 16)

            store_biases(range(9))
            pool.wait_ge(score_ready, 1)
            s = SCORE[:, P:].rearrange("p (a k) -> p a k", a=2)
            pool.affine_select(out=s, in_=s, compare_op=ALU.is_ge, fill=FUTURE, base=0,
                               pattern=[[0, 2], [-1, P]], channel_multiplier=1).then_inc(score_causal, 1)
            store_biases(range(9, 14))
            pool.wait_ge(rows_stored, 16 * 14)
            load_biases(DSA, (0, 1))
            pool.wait_ge(psum_free, 7)
            width, src = 1, S[:, 24:32, :]
            for g, w in enumerate(POOL_WINDOWS):
                dst = WINDOW[g % 2]
                t = slice(2 * g, HALF)
                step(pool.tensor_copy(dst[:, t, 0:width], src[:, t, 0:width]))
                step(pool.tensor_tensor(dst[:, t, width:], src[:, t, width:], src[:, t, 0:T - width], ALU.add))
                t = slice(2 * g, 2 * g + 2)
                pin, pooled = S[:, 24 + 2 * g:26 + 2 * g, :], S[:, 2 * g:2 * g + 2, :]
                step(pool.tensor_scalar(pooled[:, :, 16:], dst[:, t, 16:], 1.0 / w, None, ALU.mult))
                step(pool.tensor_tensor(pooled[:, :, 0:16], dst[:, t, 0:16],
                                        INV[:, g:g + 1, :].to_broadcast([P, 2, 16]), ALU.mult))
                step(pool.tensor_tensor(pooled, pooled, pin, ALU.subtract))
                width, src = w, dst
                if g == 1:
                    load_biases(DSA, (2, 3))
            pool.sem_inc(once["pooled"], 1)
            load_biases(SWA, (0, 1))
            squares(1, lambda j: (psum_free, L1_BLOCKS - 3 + j))
            load_biases(SWA, range(2, 8))
            squares(2, lambda j: (psum_free, L2_BLOCKS - 3 + j))
            load_biases(MOBA, (0, 1))
            squares(3, lambda j: (psum_free, MIX_BLOCK + 24 + 1 + j))
            squares(4, lambda j: (psum_free, MIX_BLOCK + 24 + 4 + 28 + 1 + j), 3)


def buckets(max_distance):
    n = np.arange(T)
    large = 16 + (np.log(np.maximum(n, 1).astype(np.float32) / np.float32(16))
                  / np.float32(math.log(max_distance / 16)) * np.float32(16)).astype(np.int32)
    return np.where(n < 16, n, np.minimum(large, 31))


def shape_constants():
    onehot = np.zeros((33, 3, ROWS), np.float32)
    for k, (far, window) in enumerate(((1024, T), (1024, P), (128, T))):
        b = buckets(far)
        for m in range(ROWS):
            n = T - 1 - m
            if 0 <= n < window:
                onehot[b[n], k, m] = 1.0
            else:
                onehot[32, k, m] = NEG
    const = np.zeros((P, P + 64), np.float32)
    const[:, 0:P] = np.eye(P)
    for g, w in enumerate(POOL_WINDOWS):
        const[:, P + 16 * g:P + 16 * g + 16] = 1.0 / np.minimum(np.arange(16) + 1, w)
    return onehot, const


def blocks(w, cols, tiles=None):
    w = w[:, cols]
    k, n = w.shape
    w = w.reshape(k // P, P, n)
    if tiles:
        w = w[list(tiles)]
    w = w.reshape(k // (2 * P), 2, P, n // BLK, BLK).transpose(3, 0, 2, 1, 4)
    return w.reshape(-1, P, SUB)


def paired(subs):
    order = [*range(6), *range(8, 14), 6, 7, 14, 15, *range(16, len(subs))]
    return subs[order]


def weight_stream(a):
    f = {n: np.asarray(v, np.float32)[0] for n, v in a.items() if np.ndim(v) > 2}
    r = lambda at, n: slice(at, at + n)
    w = f["even_w_in"]
    keys = np.concatenate([w[:, 3072:3200], w[:, 5248:5328], np.zeros((D, 48), np.float32)], axis=1)
    subs = [keys.reshape(4, 4, P, 256).transpose(0, 2, 1, 3).reshape(4, P, SUB)]
    subs += [blocks(w, r(at, 1024)) for at in (4224, 2048, 0, 3200, 1024)]
    pw = f["even_pool_w"].reshape(2, 2, 2, P, 256)
    subs += [pw.transpose(0, 3, 1, 2, 4).reshape(2, P, SUB), 
             paired(blocks(f["even_w_out"], r(0, 2 * BLK), L1_OUT_TILES)),
             blocks(f["even_w_out"], r(2 * BLK, 2 * BLK))]
    w = f["odd_w_in"]
    subs += [blocks(w, r(2048, 512))]
    subs += [blocks(w, r((2560 if b[0] == "g" else 0) + BLK * int(b[1]), BLK)) for b in L2_ORDER]
    subs += [paired(blocks(f["odd_w_out"], r(0, D)))]
    w = f["w_in_2"]
    subs += [blocks(w, r(2048, 1024)), blocks(w, r(0, 2048))]
    xr, gr, sb, sc, sx = (blocks(w, r(3072 + 1024 * k, 1024)) for k in range(5))
    ga, gx = (f[n].reshape(2, 4, P, P).transpose(0, 2, 1, 3).reshape(2, P, 512) for n in ("lru_wa_2", "lru_wx_2"))
    gates = np.concatenate([ga, gx], axis=2)
    subs += [xr, sc, sx, gates[:1], gr[:8], gates[1:], gr[8:], sb]
    for k, n in enumerate(("w_attn_o_2", "w_lru_o_2", "w_sc_o_2")):
        gates = blocks(w, r(8192 + D * k, D)).reshape(4, 8, P, SUB)
        outs = blocks(f[n], r(0, D)).reshape(4, 4, P, SUB)
        subs += [np.concatenate([gates, outs], axis=1).reshape(-1, P, SUB)]
    subs += [blocks(f["w_out_2"], r(0, D))]
    up = blocks(f["w_mlp_up_2"], r(0, 4 * D)).reshape(4, 32, P, SUB)
    for g in range(4):
        subs += [up[g], blocks(f["w_mlp_down_2"][D * g:D * g + D], r(0, D))]
    return np.concatenate(subs, axis=0)


def tiles(v):
    return np.asarray(v, np.float32).reshape(-1, P).T


def kernel(**a):
    import concourse.bacc as bacc
    from concourse.bass_utils import run_bass_kernel_spmd

    onehot, const = shape_constants()
    twice = lambda v: np.tile(np.asarray(v, np.float32).reshape(HD, 1), (2, 1))
    small = np.concatenate(
        [tiles(a[n][0]) for n in ("even_norm", "odd_norm", "norm_mix_g_2", "norm_mlp_g_2")]
        + [tiles(a["final_g_2"]), tiles(a["even_pool_scale"][0])]
        + [twice(a[n][0]) for n in ("even_q_gain", "even_k_gain", "odd_q_gain", "odd_k_gain")]
        + [tiles(a["gate_b_2"][0])] + [tiles(v) for v in a["lru_conv_w_2"][0]]
        + [tiles(a[n][0]) for n in ("lru_conv_b_2", "lru_ba_2", "lru_bx_2", "lru_lambda_2")]
        + [tiles(v) for v in a["sc_conv_w_2"][0]]
        + [np.broadcast_to(np.asarray(a["odd_sinks"][0], np.float32), (P, SWA_HEADS))], axis=1)
    rel, rel2 = np.asarray(a["rel_bias"], np.float32), np.asarray(a["rel_table_2"], np.float32)
    tables = np.zeros((33, 96), np.float32)
    tables[0:32, 0:16], tables[0:32, 32:64], tables[0:32, 64:72] = rel[:, 0:16], rel, rel2
    tables[32] = 1.0
    x = np.asarray(a["x"], np.float32)[0].T.reshape(NT, P, T).transpose(1, 0, 2)
    arrays = {"x": x, "w": weight_stream(a), "small": small, "tables": tables, "onehot": onehot,
              "const": const}
    arrays = {n + "_dram": np.ascontiguousarray(v, dtype=np.float32) for n, v in arrays.items()}
    nc = bacc.Bacc("TRN2", target_bir_lowering=False, num_devices=1)
    ins = [nc.dram_tensor(n, v.shape, F32, kind="ExternalInput").ap() for n, v in arrays.items()]
    out = nc.dram_tensor("y_dram", [P, NT, T], F32, kind="ExternalOutput").ap()
    build(nc, *ins, out)
    r = run_bass_kernel_spmd(nc, [arrays], core_ids=[0])
    y = r.results[0]["y_dram"]
    return np.ascontiguousarray(y.transpose(2, 1, 0)).reshape(1, T, D)
```
